# Optimizing a Trainium2 kernel written in Bass

```python
import jax, jax.numpy as jnp
from jax import lax
import numpy as np
import jax
import jax.numpy as jnp

D_MODEL = 1024
BATCH = 1
SEQ = 512
DEPTH = 1

HEAD_DIM = 64
ATTN_HEADS = 8
ATTN_WIDTH = ATTN_HEADS * HEAD_DIM
ROPE_DIM = HEAD_DIM // 4
ROPE_THETA = 500000.0
DILATED_PATTERNS = ((128, 1), (512, 4), (2048, 16))
HG_HEADS = 4
HG_EXPAND = 128
HG_VDIM = 128
HG_KDIM = HG_HEADS * HG_EXPAND
HG_WIDTH = HG_HEADS * HG_VDIM
HG_CHUNK = 64
MIX_WIDTH = ATTN_WIDTH + HG_WIDTH
IN_SIZES = (ATTN_WIDTH, ATTN_WIDTH, ATTN_WIDTH, HG_KDIM, HG_KDIM, HG_WIDTH, HG_WIDTH)
IN_COLS = sum(IN_SIZES)
D_FF = 2816
EPS = 1e-6
NEG_INF = -1e30


def _rms_norm(x, w):
    xf = x.astype(jnp.float32)
    y = xf * lax.rsqrt(jnp.mean(xf * xf, axis=-1, keepdims=True) + EPS)
    return (y * w.astype(jnp.float32)).astype(x.dtype)

def _swiglu(h, w1, w3, w2):
    return (jax.nn.silu(h @ w1) * (h @ w3)) @ w2

def _rope_tables(s):
    inv = ROPE_THETA ** (-jnp.arange(0, ROPE_DIM, 2, dtype=jnp.float32) / ROPE_DIM)
    ang = jnp.arange(s, dtype=jnp.float32)[:, None] * inv[None, :]
    return jnp.cos(ang), jnp.sin(ang)

def _partial_rope(x, cos, sin):
    half = ROPE_DIM // 2
    xf = x.astype(jnp.float32)
    x1, x2, rest = xf[..., :half], xf[..., half:ROPE_DIM], xf[..., ROPE_DIM:]
    c, s_ = cos[None, :, None, :], sin[None, :, None, :]
    out = jnp.concatenate([x1 * c - x2 * s_, x1 * s_ + x2 * c, rest], axis=-1)
    return out.astype(x.dtype)

def _dilated_branch(q, k, v, window, dilation):
    b, s, h, dh = q.shape
    w = window // dilation
    l = s // dilation
    nb = -(-l // w)
    lp = nb * w
    bb = b * dilation

    def to_sub(t):
        t = t.reshape(b, l, dilation, h, dh).transpose(0, 2, 1, 3, 4).reshape(bb, l, h, dh)
        return jnp.pad(t, ((0, 0), (0, lp - l), (0, 0), (0, 0)))

    def windows(t):
        t = jnp.pad(t, ((0, 0), (w, 0), (0, 0), (0, 0))).reshape(bb, nb + 1, w, h, dh)
        return jnp.concatenate([t[:, :-1], t[:, 1:]], axis=2)

    qb = to_sub(q).reshape(bb, nb, w, h, dh)
    kw, vw = windows(to_sub(k)), windows(to_sub(v))
    scores = jnp.einsum('bnqhd,bnkhd->bnhqk', qb, kw,
                        preferred_element_type=jnp.float32) * (dh ** -0.5)
    qi = jnp.arange(w)[:, None]
    kj = jnp.arange(2 * w)[None, :]
    dist = qi + w - kj
    band = (dist >= 0) & (dist <= w)
    valid = band[None] & ((jnp.arange(nb)[:, None, None] > 0) | (kj >= w)[None])
    scores = jnp.where(valid[None, :, None], scores, NEG_INF)
    m = jnp.max(scores, axis=-1, keepdims=True)
    p = jnp.exp(scores - m)
    den = jnp.sum(p, axis=-1, keepdims=True)
    out = jnp.einsum('bnhqk,bnkhd->bnqhd', p / den, vw.astype(jnp.float32))
    lse = (m + jnp.log(den))[..., 0]
    out = (out.reshape(bb, lp, h, dh)[:, :l]
           .reshape(b, dilation, l, h, dh).transpose(0, 2, 1, 3, 4).reshape(b, s, h, dh))
    lse = (lse.transpose(0, 1, 3, 2).reshape(bb, lp, h)[:, :l]
           .reshape(b, dilation, l, h).transpose(0, 2, 1, 3).reshape(b, s, h))
    return out, lse

def _dilated_attention(q, k, v):
    outs, lses = [], []
    for window, dilation in DILATED_PATTERNS:
        o, lse = _dilated_branch(q, k, v, window, dilation)
        outs.append(o)
        lses.append(lse)
    wts = jax.nn.softmax(jnp.stack(lses), axis=0)
    return jnp.einsum('pbsh,pbshd->bshd', wts, jnp.stack(outs))

def _hgrn2(q, f_pre, inp, lb):
    b, s, h, n = q.shape
    dv = inp.shape[-1]
    c = HG_CHUNK
    nc = s // c
    lb = lb.reshape(h, n).astype(jnp.float32)
    f = lb + (1.0 - lb) * jax.nn.sigmoid(f_pre.astype(jnp.float32))
    g = jnp.log(f)
    k = 1.0 - f

    def chunks(t):
        return t.reshape(b, nc, c, h, t.shape[-1]).transpose(0, 3, 1, 2, 4)

    qc, kc, gc, vc = chunks(q.astype(jnp.float32)), chunks(k), chunks(g), chunks(inp.astype(jnp.float32))
    G = jnp.cumsum(gc, axis=3)
    G_last = G[:, :, :, -1:]
    q_dec = qc * jnp.exp(G)
    att = jnp.einsum('bhntk,bhnsk->bhnts', q_dec, kc * jnp.exp(-G))
    att = jnp.where(jnp.tril(jnp.ones((c, c), dtype=bool)), att, 0.0)
    intra = jnp.einsum('bhnts,bhnsv->bhntv', att, vc)
    chunk_state = jnp.einsum('bhnsk,bhnsv->bhnkv', kc * jnp.exp(G_last - G), vc)
    decay = jnp.exp(G_last[:, :, :, 0])

    def step(state, xs):
        dec, upd = xs
        return dec[..., None] * state + upd, state

    _, prev = lax.scan(step, jnp.zeros((b, h, n, dv), jnp.float32),
                       (jnp.moveaxis(decay, 2, 0), jnp.moveaxis(chunk_state, 2, 0)))
    prev = jnp.moveaxis(prev, 0, 2)
    inter = jnp.einsum('bhntk,bhnkv->bhntv', q_dec, prev)
    return (intra + inter).transpose(0, 2, 3, 1, 4).reshape(b, s, h, dv)

def first_inputs(seed: int = 0) -> dict:
    key = jax.random.key(seed)
    ks = jax.random.split(key, 20)
    f32 = jnp.float32

    def nrm(k, shape, fan_in):
        return jax.random.normal(k, shape, f32) * (fan_in ** -0.5)

    def gain(k, shape):
        return 1.0 + 0.02 * jax.random.normal(k, shape, f32)

    return {
        'x': jax.random.normal(ks[0], (BATCH, SEQ, D_MODEL), f32),
        'ffn1_norm': gain(ks[1], (DEPTH, D_MODEL)),
        'ffn1_w1': nrm(ks[2], (DEPTH, D_MODEL, D_FF), D_MODEL),
        'ffn1_w3': nrm(ks[3], (DEPTH, D_MODEL, D_FF), D_MODEL),
        'ffn1_w2': nrm(ks[4], (DEPTH, D_FF, D_MODEL), D_FF),
        'mix_norm': gain(ks[5], (DEPTH, D_MODEL)),
        'w_in': nrm(ks[6], (DEPTH, D_MODEL, IN_COLS), D_MODEL),
        'q_norm': gain(ks[7], (DEPTH, HEAD_DIM)),
        'k_norm': gain(ks[8], (DEPTH, HEAD_DIM)),
        'hg_lb_logits': 0.1 * jax.random.normal(ks[9], (DEPTH + 1, HG_KDIM), f32),
        'hg_out_norm': gain(ks[10], (DEPTH, HG_VDIM)),
        'w_out': nrm(ks[11], (DEPTH, MIX_WIDTH, D_MODEL), MIX_WIDTH),
        'ffn2_norm': gain(ks[12], (DEPTH, D_MODEL)),
        'ffn2_w1': nrm(ks[13], (DEPTH, D_MODEL, D_FF), D_MODEL),
        'ffn2_w3': nrm(ks[14], (DEPTH, D_MODEL, D_FF), D_MODEL),
        'ffn2_w2': nrm(ks[15], (DEPTH, D_FF, D_MODEL), D_FF),
    }

def first_block(x, ffn1_norm, ffn1_w1, ffn1_w3, ffn1_w2, mix_norm, w_in, q_norm, k_norm,
              hg_lb_logits, hg_out_norm, w_out, ffn2_norm, ffn2_w1, ffn2_w3, ffn2_w2):
    b, s, _ = x.shape
    cos, sin = _rope_tables(s)
    lower_bounds = jnp.cumsum(jax.nn.softmax(hg_lb_logits.astype(jnp.float32), axis=0), axis=0)
    split_at = list(np.cumsum(IN_SIZES)[:-1])
    for layer in range(DEPTH):
        x = x + 0.5 * _swiglu(_rms_norm(x, ffn1_norm[layer]),
                              ffn1_w1[layer], ffn1_w3[layer], ffn1_w2[layer])
        h = _rms_norm(x, mix_norm[layer])
        proj = h @ w_in[layer]
        aq, ak, av, hq, hf, hi, hg = jnp.split(proj, split_at, axis=-1)
        aq = _partial_rope(_rms_norm(aq.reshape(b, s, ATTN_HEADS, HEAD_DIM), q_norm[layer]), cos, sin)
        ak = _partial_rope(_rms_norm(ak.reshape(b, s, ATTN_HEADS, HEAD_DIM), k_norm[layer]), cos, sin)
        av = av.reshape(b, s, ATTN_HEADS, HEAD_DIM)
        attn_out = _dilated_attention(aq, ak, av).astype(x.dtype).reshape(b, s, ATTN_WIDTH)
        rec = _hgrn2(hq.reshape(b, s, HG_HEADS, HG_EXPAND), hf.reshape(b, s, HG_HEADS, HG_EXPAND),
                     hi.reshape(b, s, HG_HEADS, HG_VDIM), lower_bounds[layer]).astype(x.dtype)
        rec = _rms_norm(rec, hg_out_norm[layer]) * jax.nn.silu(hg.reshape(b, s, HG_HEADS, HG_VDIM))
        mixed = jnp.concatenate([attn_out, rec.reshape(b, s, HG_WIDTH)], axis=-1)
        x = x + mixed @ w_out[layer]
        x = x + 0.5 * _swiglu(_rms_norm(x, ffn2_norm[layer]),
                              ffn2_w1[layer], ffn2_w3[layer], ffn2_w2[layer])
    return x


DEPTH_2 = 2

N_HEADS = 8
N_KV = 2
HPG = N_HEADS // N_KV
ATTN_W = N_HEADS * HEAD_DIM
KV_W = N_KV * HEAD_DIM
CONV_CH = D_MODEL - ATTN_W
CONV_W = 3
D_MIX = ATTN_W + CONV_CH
CMP_BLOCK = 32
CMP_STRIDE = 16
CMP_HIDDEN = 256
SEL_BLOCK = 64
SEL_TOPN = 16
WINDOW = 512
WIN_QBLOCK = 128
SEL_QCHUNK = 64
N_EXPERTS = 8
TOP_K = 2
D_FF_EXPERT = 1408
N_DENSE = (DEPTH_2 + 1) // 2
N_MOE = DEPTH_2 // 2
ALPHA = (2 * DEPTH_2) ** 0.25
BETA = (8 * DEPTH_2) ** -0.25
LN_EPS = 1e-5
NEG = -1e30
FORCE = 1e9
SPLIT_WIDTHS = (ATTN_W, KV_W, KV_W, KV_W, KV_W, KV_W, KV_W, 3 * N_HEADS, CONV_CH, CONV_CH, CONV_CH)
D_IN = sum(SPLIT_WIDTHS)


def layer_norm(x, g, b):
    xf = x.astype(jnp.float32)
    mu = jnp.mean(xf, -1, keepdims=True)
    var = jnp.mean(jnp.square(xf - mu), -1, keepdims=True)
    return ((xf - mu) * lax.rsqrt(var + LN_EPS) * g + b).astype(x.dtype)

def compress(k, pos, w1, b1, w2, b2):
    bsz, g, s, dh = k.shape
    ratio = CMP_BLOCK // CMP_STRIDE
    n_cmp = s // CMP_STRIDE - ratio + 1
    blocks = k.reshape(bsz, g, s // CMP_STRIDE, CMP_STRIDE, dh)
    win = jnp.concatenate([blocks[:, :, r:r + n_cmp] for r in range(ratio)], axis=3)
    win = (win + pos).reshape(bsz, g, n_cmp, CMP_BLOCK * dh)
    return jax.nn.gelu(win @ w1 + b1) @ w2 + b2

def cmp_attention(q, kc, vc):
    s_len = q.shape[3]
    n = kc.shape[2]
    t = jnp.arange(s_len)
    ends = jnp.arange(n) * CMP_STRIDE + CMP_BLOCK - 1
    mask = ends[None, :] <= t[:, None]
    sc = jnp.einsum('bghsd,bgnd->bghsn', q, kc).astype(jnp.float32) * HEAD_DIM ** -0.5
    p = jax.nn.softmax(jnp.where(mask, sc, NEG), axis=-1) * mask
    o = jnp.einsum('bghsn,bgnd->bghsd', p.astype(vc.dtype), vc)
    return o, p

def select_blocks(p_cmp, s_len):
    n = p_cmp.shape[-1]
    n_sel = s_len // SEL_BLOCK
    cs = jnp.arange(n) * CMP_STRIDE
    ss = jnp.arange(n_sel) * SEL_BLOCK
    overlap = ((cs[:, None] < ss[None, :] + SEL_BLOCK) & (cs[:, None] + CMP_BLOCK > ss[None, :])).astype(jnp.float32)
    imp = jnp.einsum('bghsn,nj->bgsj', p_cmp, overlap)
    t = jnp.arange(s_len)[:, None]
    j = jnp.arange(n_sel)[None, :]
    cur = t // SEL_BLOCK
    valid = j * SEL_BLOCK <= t
    forced = (j == 0) | (j == cur) | (j == cur - 1)
    score = jnp.where(forced, FORCE, jnp.where(valid, imp, NEG))
    _, idx = lax.top_k(score, min(SEL_TOPN, n_sel))
    return idx

def sel_attention(q, ks, vs, idx):
    bsz, g, hpg, s_len, dh = q.shape
    n_sel = s_len // SEL_BLOCK
    k_top = idx.shape[-1]
    nc = s_len // SEL_QCHUNK
    kb = ks.reshape(bsz, g, n_sel, SEL_BLOCK, dh)
    vb = vs.reshape(bsz, g, n_sel, SEL_BLOCK, dh)
    qc = q.reshape(bsz, g, hpg, nc, SEL_QCHUNK, dh).transpose(3, 0, 1, 2, 4, 5)
    ic = idx.reshape(bsz, g, nc, SEL_QCHUNK, k_top).transpose(2, 0, 1, 3, 4)
    starts = jnp.arange(nc) * SEL_QCHUNK
    gather = jax.vmap(jax.vmap(lambda blk, ix: blk[ix]))

    def chunk(args):
        qq, ii, start = args
        kg = gather(kb, ii)
        vg = gather(vb, ii)
        sc = jnp.einsum('bghqd,bgqkrd->bghqkr', qq, kg).astype(jnp.float32) * HEAD_DIM ** -0.5
        pos = ii[..., None] * SEL_BLOCK + jnp.arange(SEL_BLOCK)
        tq = start + jnp.arange(SEL_QCHUNK)
        mask = (pos <= tq[None, None, :, None, None])[:, :, None]
        sc = jnp.where(mask, sc, NEG).reshape(bsz, g, hpg, SEL_QCHUNK, k_top * SEL_BLOCK)
        p = jax.nn.softmax(sc, axis=-1).reshape(bsz, g, hpg, SEL_QCHUNK, k_top, SEL_BLOCK)
        return jnp.einsum('bghqkr,bgqkrd->bghqd', p.astype(vg.dtype), vg)

    o = lax.map(chunk, (qc, ic, starts))
    return o.transpose(1, 2, 3, 0, 4, 5).reshape(bsz, g, hpg, s_len, dh)

def win_attention(q, kw, vw):
    bsz, g, hpg, s_len, dh = q.shape
    nb = s_len // WIN_QBLOCK
    span = WINDOW // WIN_QBLOCK
    ksz = (span + 1) * WIN_QBLOCK
    padw = ((0, 0), (0, 0), (WINDOW, 0), (0, 0))
    kp = jnp.pad(kw, padw).reshape(bsz, g, nb + span, WIN_QBLOCK, dh)
    vp = jnp.pad(vw, padw).reshape(bsz, g, nb + span, WIN_QBLOCK, dh)
    kband = jnp.concatenate([kp[:, :, i:i + nb] for i in range(span + 1)], axis=3)
    vband = jnp.concatenate([vp[:, :, i:i + nb] for i in range(span + 1)], axis=3)
    qb = q.reshape(bsz, g, hpg, nb, WIN_QBLOCK, dh)
    sc = jnp.einsum('bghnqd,bgnkd->bghnqk', qb, kband).astype(jnp.float32) * HEAD_DIM ** -0.5
    blk = jnp.arange(nb)[:, None, None] * WIN_QBLOCK
    tq = blk + jnp.arange(WIN_QBLOCK)[None, :, None]
    sk = blk - WINDOW + jnp.arange(ksz)[None, None, :]
    mask = (sk <= tq) & (tq - sk < WINDOW) & (sk >= 0)
    p = jax.nn.softmax(jnp.where(mask, sc, NEG), axis=-1)
    o = jnp.einsum('bghnqk,bgnkd->bghnqd', p.astype(vband.dtype), vband)
    return o.reshape(bsz, g, hpg, s_len, dh)

def short_conv(u, b_gate, c_gate, w):
    s_len = u.shape[1]
    z = jnp.pad(c_gate * u, ((0, 0), (CONV_W - 1, 0), (0, 0)))
    y = z[:, 0:s_len] * w[0]
    for i in range(1, CONV_W):
        y = y + z[:, i:i + s_len] * w[i]
    return b_gate * y

def hybrid_mixer(h, w_in, cmp_pos, cmp_w1, cmp_b1, cmp_w2, cmp_b2, conv_w, w_o):
    bsz, s_len, _ = h.shape
    z = h @ w_in
    offsets = np.cumsum(SPLIT_WIDTHS)[:-1].tolist()
    q, kc, vc, ks, vs, kw, vw, gates, u, bg, cg = jnp.split(z, offsets, axis=-1)
    q = q.reshape(bsz, s_len, N_KV, HPG, HEAD_DIM).transpose(0, 2, 3, 1, 4)

    def kv(t):
        return t.reshape(bsz, s_len, N_KV, HEAD_DIM).transpose(0, 2, 1, 3)

    kc_c = compress(kv(kc), cmp_pos[0], cmp_w1[0], cmp_b1[0], cmp_w2[0], cmp_b2[0])
    vc_c = compress(kv(vc), cmp_pos[1], cmp_w1[1], cmp_b1[1], cmp_w2[1], cmp_b2[1])
    o_cmp, p_cmp = cmp_attention(q, kc_c, vc_c)
    idx = select_blocks(p_cmp, s_len)
    o_sel = sel_attention(q, kv(ks), kv(vs), idx)
    o_win = win_attention(q, kv(kw), kv(vw))
    g = jax.nn.sigmoid(gates).reshape(bsz, s_len, 3, N_KV, HPG).transpose(2, 0, 3, 4, 1)[..., None]
    o_attn = g[0] * o_cmp + g[1] * o_sel + g[2] * o_win
    o_attn = o_attn.transpose(0, 3, 1, 2, 4).reshape(bsz, s_len, ATTN_W)
    o_conv = short_conv(u, bg, cg, conv_w)
    return jnp.concatenate([o_attn, o_conv], axis=-1) @ w_o

def swiglu(h, wg, wu, wd):
    return (jax.nn.silu(h @ wg) * (h @ wu)) @ wd

def moe_swiglu(h, w_router, wg, wu, wd):
    logits = (h @ w_router).astype(jnp.float32)
    top_v, top_i = lax.top_k(logits, TOP_K)
    w_top = jax.nn.softmax(top_v, axis=-1)
    gate = jnp.sum(jax.nn.one_hot(top_i, N_EXPERTS, dtype=jnp.float32) * w_top[..., None], axis=-2)
    out = jnp.zeros_like(h)
    for e in range(N_EXPERTS):
        out = out + gate[..., e:e + 1].astype(h.dtype) * swiglu(h, wg[e], wu[e], wd[e])
    return out

def second_inputs(seed: int = 0) -> dict:
    key = jax.random.key(seed)
    ks = jax.random.split(key, 24)

    def nrm(k, shape, scale):
        return jax.random.normal(k, shape, jnp.float32) * scale

    return {
        'x': nrm(ks[0], (BATCH, SEQ, D_MODEL), 1.0),
        'ln_in_g': 1.0 + nrm(ks[1], (D_MODEL,), 0.02),
        'ln_in_b': nrm(ks[2], (D_MODEL,), 0.02),
        'w_in': nrm(ks[3], (DEPTH_2, D_MODEL, D_IN), D_MODEL ** -0.5),
        'cmp_pos': nrm(ks[4], (DEPTH_2, 2, CMP_BLOCK, HEAD_DIM), 0.1),
        'cmp_w1': nrm(ks[5], (DEPTH_2, 2, CMP_BLOCK * HEAD_DIM, CMP_HIDDEN), (CMP_BLOCK * HEAD_DIM) ** -0.5),
        'cmp_b1': nrm(ks[6], (DEPTH_2, 2, CMP_HIDDEN), 0.02),
        'cmp_w2': nrm(ks[7], (DEPTH_2, 2, CMP_HIDDEN, HEAD_DIM), CMP_HIDDEN ** -0.5),
        'cmp_b2': nrm(ks[8], (DEPTH_2, 2, HEAD_DIM), 0.02),
        'conv_w': nrm(ks[9], (DEPTH_2, CONV_W, CONV_CH), CONV_W ** -0.5),
        'w_o': nrm(ks[10], (DEPTH_2, D_MIX, D_MODEL), BETA * D_MIX ** -0.5),
        'ln1_g': 1.0 + nrm(ks[11], (DEPTH_2, D_MODEL), 0.02),
        'ln1_b': nrm(ks[12], (DEPTH_2, D_MODEL), 0.02),
        'ln2_g': 1.0 + nrm(ks[13], (DEPTH_2, D_MODEL), 0.02),
        'ln2_b': nrm(ks[14], (DEPTH_2, D_MODEL), 0.02),
        'ffn_wg': nrm(ks[15], (N_DENSE, D_MODEL, D_FF), D_MODEL ** -0.5),
        'ffn_wu': nrm(ks[16], (N_DENSE, D_MODEL, D_FF), D_MODEL ** -0.5),
        'ffn_wd': nrm(ks[17], (N_DENSE, D_FF, D_MODEL), BETA * D_FF ** -0.5),
        'moe_router': nrm(ks[18], (N_MOE, D_MODEL, N_EXPERTS), D_MODEL ** -0.5),
        'moe_wg': nrm(ks[19], (N_MOE, N_EXPERTS, D_MODEL, D_FF_EXPERT), D_MODEL ** -0.5),
        'moe_wu': nrm(ks[20], (N_MOE, N_EXPERTS, D_MODEL, D_FF_EXPERT), D_MODEL ** -0.5),
        'moe_wd': nrm(ks[21], (N_MOE, N_EXPERTS, D_FF_EXPERT, D_MODEL), BETA * D_FF_EXPERT ** -0.5),
    }

def second_block(x, ln_in_g, ln_in_b, w_in, cmp_pos, cmp_w1, cmp_b1, cmp_w2, cmp_b2, conv_w, w_o,
              ln1_g, ln1_b, ln2_g, ln2_b, ffn_wg, ffn_wu, ffn_wd,
              moe_router, moe_wg, moe_wu, moe_wd):
    h = layer_norm(x, ln_in_g, ln_in_b)
    for l in range(DEPTH_2):
        m = hybrid_mixer(h, w_in[l], cmp_pos[l], cmp_w1[l], cmp_b1[l], cmp_w2[l], cmp_b2[l],
                         conv_w[l], w_o[l])
        h = layer_norm(ALPHA * h + m, ln1_g[l], ln1_b[l])
        if l % 2 == 0:
            f = swiglu(h, ffn_wg[l // 2], ffn_wu[l // 2], ffn_wd[l // 2])
        else:
            f = moe_swiglu(h, moe_router[l // 2], moe_wg[l // 2], moe_wu[l // 2], moe_wd[l // 2])
        h = layer_norm(ALPHA * h + f, ln2_g[l], ln2_b[l])
    return h


def setup_inputs(seed=0):
    out = dict(first_inputs(seed))
    for name, value in second_inputs(seed + 1).items():
        if name != "x":
            out[name + "_2"] = value
    return out


def reference(
    x, ffn1_norm, ffn1_w1, ffn1_w3, ffn1_w2, mix_norm, w_in, q_norm, k_norm, hg_lb_logits,
    hg_out_norm, w_out, ffn2_norm, ffn2_w1, ffn2_w3, ffn2_w2, ln_in_g_2, ln_in_b_2, w_in_2,
    cmp_pos_2, cmp_w1_2, cmp_b1_2, cmp_w2_2, cmp_b2_2, conv_w_2, w_o_2, ln1_g_2, ln1_b_2,
    ln2_g_2, ln2_b_2, ffn_wg_2, ffn_wu_2, ffn_wd_2, moe_router_2, moe_wg_2, moe_wu_2, moe_wd_2,
):
    x = first_block(
        x, ffn1_norm, ffn1_w1, ffn1_w3, ffn1_w2, mix_norm, w_in, q_norm, k_norm, hg_lb_logits,
        hg_out_norm, w_out, ffn2_norm, ffn2_w1, ffn2_w3, ffn2_w2,
    )
    return second_block(
        x, ln_in_g_2, ln_in_b_2, w_in_2, cmp_pos_2, cmp_w1_2, cmp_b1_2, cmp_w2_2, cmp_b2_2,
        conv_w_2, w_o_2, ln1_g_2, ln1_b_2, ln2_g_2, ln2_b_2, ffn_wg_2, ffn_wu_2, ffn_wd_2,
        moe_router_2, moe_wg_2, moe_wu_2, moe_wd_2,
    )


_drawn_inputs = setup_inputs


def setup_inputs(seed=0):
    import zlib

    import numpy as np

    out = dict(_drawn_inputs(seed))
    spreads = {}
    factors = {'ffn1_norm': 3.188,
     'q_norm': 8.0,
     'k_norm': 8.0,
     'hg_out_norm': 4.497,
     'ffn2_norm': 5.525,
     'cmp_pos_2': 5.023,
     'cmp_b1_2': 8.0,
     'cmp_b2_2': 8.0}
    for name, (base, spread) in spreads.items():
        noise = np.random.default_rng([zlib.crc32(name.encode()), seed]).standard_normal(out[name].shape)
        drawn = base * np.exp(spread * noise) if base else spread * noise
        out[name] = jnp.asarray(drawn.astype(out[name].dtype))
    for name, factor in factors.items():
        out[name] = (out[name] * factor).astype(out[name].dtype)
    return out
```

```python
from contextlib import ExitStack

import numpy as np
import concourse.bass as bass
from concourse import mybir

F32 = mybir.dt.float32
F32R = mybir.dt.float32r
I32 = mybir.dt.int32
U32 = mybir.dt.uint32
ALU = mybir.AluOpType
ACT = mybir.ActivationFunctionType
AX = mybir.AxisListType

P = 128
S = 512
NT = S // P
D = 1024
KD = D // P
FF = 2816 // P
FF_PARTS = (12, 10)
HD = 64
HEADS = 8
SCALE = float(HD) ** -0.5
EPS = 1e-6
LN_EPS = 1e-5
NEG = -1e30
LN_EXP = "natural_log_exp_and_others"
CHUNK = 64
NCHUNK = S // CHUNK
NQKV = 20
NCMP = S // 16 - 1
ALPHA = 4.0 ** 0.25
NE = 8
FE = 1408 // P
CAP = 160
WIDE = 256
JT = (P, CAP - P)
BLOCKS = -(-S // CAP)
EXTRA = (2 * S - NE) // CAP
PLAN = 16
WIN = 4 * NCMP
TILE = P * P // P
DOWN = ((0, 2), (2, 2), (4, 2), (6, 1), (7, 1))
NI = FE + len(DOWN)
SLOT = 24 * TILE
ITEM = 16 * TILE

IDENT, ONES_D, ONES_H, ROT, SEL0, SEL1, HMASK = (P * i for i in range(7))
NCONST = 7 * P


def vector_columns():
    at, col = 0, {}
    names = [("ffn1_norm", 8), ("mix_norm", 8), ("ffn2_norm", 8), ("q_norm", 1), ("k_norm", 1),
             ("hg_out_norm", 1), ("lb_logits", 8), ("ln_in_g", 8), ("ln_in_b", 8)]
    for l in range(2):
        names += [(f"ln1_g{l}", 8), (f"ln1_b{l}", 8), (f"ln2_g{l}", 8), (f"ln2_b{l}", 8),
                  (f"conv{l}", 12), (f"cmp_b1{l}", 4), (f"cmp_b2k{l}", 1)]
    for name, n in names:
        col[name] = (at, n)
        at += n
    return col, at


VCOL, NVEC = vector_columns()


def stream_plan(stop):
    sizes, first = [], {}

    def stage(name, item_sizes):
        first[name] = len(sizes)
        sizes.extend(item_sizes)

    def ffn(name):
        for part, n in enumerate(FF_PARTS):
            stage(f"{name}_up{part}", [ITEM] * n)
            stage(f"{name}_down{part}", [2 * n * TILE] * 4)

    ffn("ffn1")
    stage("in0", [ITEM] * (NQKV // 2))
    stage("tok0", [ITEM] * 4)
    stage("out0", [ITEM] * 4)
    ffn("ffn2")
    if stop != "block1":
        for l in (1, 2):
            stage(f"in{l}", [ITEM] * (NQKV // 2))
            stage(f"tok{l}", [KD * 280])
            stage(f"cmp{l}", [ITEM] * 4)
            stage(f"out{l}", [ITEM] * 4)
            if l == 1:
                ffn("ffn3")
                if stop == "layer1":
                    break
    return sizes, first


def build(nc, t, out, stop="all"):
    sizes, first = stream_plan(stop)
    full = stop == "all"
    with ExitStack() as ctx:
        def sb(name, shape, dt=F32, on=ctx):
            return on.enter_context(nc.sbuf_tensor(name, shape, dt))

        def sem(name):
            return ctx.enter_context(nc.semaphore(name))

        consts = sb("consts", [P, NCONST])
        vecs = sb("vecs", [P, NVEC])
        xh = sb("xh", [P, KD, S], F32R)
        xl = sb("xl", [P, KD, S], F32R)

        stack1 = ExitStack()
        xT = sb("xT", [P, KD, S], on=stack1)
        raw = sb("raw", [P, 2, SLOT], on=stack1)
        wh = sb("wh", [P, 2, SLOT], F32R, on=stack1)
        wl = sb("wl", [P, 2, SLOT], F32R, on=stack1)

        with ExitStack() as ffn_scope:
            ah = sb("ah", [P, max(FF_PARTS), S], F32R, on=ffn_scope)
            al = sb("al", [P, max(FF_PARTS), S], F32R, on=ffn_scope)
            silu_t = sb("silu_t", [P, 2, S], on=ffn_scope)
            gated = sb("gated", [P, 2, S], on=ffn_scope)
            sq = sb("sq", [P, 4, S], on=ffn_scope)
            rstd = sb("rstd", [P, S], on=ffn_scope)
            normed = sb("normed", [P, 2, S], on=ffn_scope)
        with ExitStack() as mid:
            proj = sb("proj", [P, NQKV, S], on=mid)
            with ExitStack() as mid1:
                vtok = sb("vtok", [P, 2, NT, 256], on=mid1)
                itok = sb("itok", [P, 2, NT, 256], on=mid1)
                mask1 = sb("mask1", [P, S], on=mid1)
                rope = sb("rope", [P, 2, S], on=mid1)
                reset = sb("reset", [P, S], on=mid1)
                lbv = sb("lbv", [P, 8, 4], on=mid1)
                decay = sb("decay", [P, 4, NCHUNK], on=mid1)
                with ExitStack() as gate_scope:
                    hG = sb("hG", [P, 2, 2 * S], on=gate_scope)
                    hE = sb("hE", [P, 2, 2 * S], on=gate_scope)
                with ExitStack() as at_scope:
                    sc1 = sb("sc1", [P, 3, S], on=at_scope)
                    pt1 = sb("pt1", [P, 3, S], on=at_scope)
                    st1 = sb("st1", [P, 3, 8], on=at_scope)
                    rn = sb("rn", [P, 2, S], on=at_scope)
                with ExitStack() as hg_scope:
                    att = sb("att", [P, 2, NT, P], on=hg_scope)
                    ktok = sb("ktok", [P, 2, NT, P], on=hg_scope)
                    states = sb("states", [P, NCHUNK - 1, P], on=hg_scope)
                    hn = sb("hn", [P, 3, S], on=hg_scope)
            with ExitStack() as mid2:
                vgate = sb("vgate", [P, NT, 280], on=mid2)
                kdup = sb("kdup", [P, 4, S], on=mid2)
                mask2 = sb("mask2", [P, S], on=mid2)
                cmask = sb("cmask", [P, 2, NT * NCMP], on=mid2)
                cmpw = sb("cmpw", [P, 480], on=mid2)
                hid = sb("hid", [P, 2, 2, 2 * NCMP], on=mid2)
                kcT = sb("kcT", [P, 2 * NCMP], on=mid2)
                vcT = sb("vcT", [P, 2, HD], on=mid2)
                with ExitStack() as win_scope:
                    win = sb("win", [P, 2, 16 * WIN + WIDE - WIN], F32R, on=win_scope)
                    wnf = sb("wnf", [P, 16, 2, NCMP], on=win_scope)
                with ExitStack() as at_scope:
                    sc2 = sb("sc2", [P, 3, S], on=at_scope)
                    pt2 = sb("pt2", [P, 3, S], on=at_scope)
                    st2 = sb("st2", [P, 3, 8], on=at_scope)
                    cs = sb("cs", [P, 2, 2, 2, NT, NCMP], on=at_scope)
                    ptc = sb("ptc", [P, 2, S], on=at_scope)
                    cst = sb("cst", [P, 2, 3, 16], on=at_scope)
        stack1.close()
        with ExitStack() as moe:
            yh = sb("yh", [P, 2, D], F32R, on=moe)
            yl = sb("yl", [P, 2, D], F32R, on=moe)
            acc = sb("acc", [P, NT, D], on=moe)
            raw_m = sb("raw_m", [P, 4, 2 * FE * TILE], on=moe)
            wmh = sb("wmh", [P, 2, 2 * FE * TILE], F32R, on=moe)
            wml = sb("wml", [P, 2, 2 * FE * TILE], F32R, on=moe)
            pick = sb("pick", [P, NT, WIDE], F32R, on=moe)
            pickT = sb("pickT", [P, 2, S], F32R, on=moe)
            xg = sb("xg", [P, KD, 2, CAP], F32R, on=moe)
            yf = sb("yf", [P, KD, CAP], on=moe)
            part = sb("part", [P, 2, 2, CAP], on=moe)
            both = sb("both", [P, 2, 2, CAP], on=moe)
            glu_t = sb("glu_t", [P, 2, CAP], on=moe)
            glu = sb("glu", [P, 2, CAP], on=moe)
            gg = sb("gg", [P, FE, 2, CAP], F32R, on=moe)
            mtab = sb("mtab", [P, WIDE + 2 * P + NE + KD * NE], on=moe)
            rt = sb("rt", [P, 6, NT * NE], on=moe)
            top_at = sb("top_at", [P, NT, NE], U32, on=moe)
            pair = sb("pair", [P, 4, NT], on=moe)
            picked = sb("picked", [P, NT, NE], on=moe)
            gates = sb("gates", [P, NE, NT], on=moe)
            ranks = sb("ranks", [P, BLOCKS * NE, NT], on=moe)
            rank_col = sb("rank_col", [P, NT], on=moe)
            gate_col = sb("gate_col", [P, NT], on=moe)
            gate_row = sb("gate_row", [P, 2], on=moe)
            over = sb("over", [1, 4, (BLOCKS - 1) * NE], on=moe)
            match = sb("match", [1, 2, EXTRA, (BLOCKS - 1) * NE], on=moe)
            plan_f = sb("plan_f", [1, 2, PLAN], on=moe)
            plan = sb("plan", [1, 2, PLAN], I32, on=moe)
            bn = sb("bn", [P, NT, 2, 6], on=moe)
            mv = sb("mv", [P, NT, 4], on=moe)
        ps = ctx.enter_context(nc.psum_tensor("ps", [P, 8, S], F32))

        ident = consts[:, IDENT:IDENT + P]

        def vec(name):
            at, n = VCOL[name]
            return vecs[:, at:at + n]

        raw_loaded = [sem("raw_loaded0"), sem("raw_loaded1")]
        hi_ready, lo_ready, item_done, evac_done = (sem(n) for n in ("hi_ready", "lo_ready", "item_done", "evac_done"))
        consts_loaded, x_loaded, stored = sem("consts_loaded"), sem("x_loaded"), sem("stored")
        silu_ready, hidden_hi, hidden_lo = sem("silu_ready"), sem("hidden_hi"), sem("hidden_lo")
        x_hi, x_lo = sem("x_hi"), sem("x_lo")
        act_chain, dve_chain = sem("act_chain"), sem("dve_chain")
        n_sq, n_stat, n_rstd, n_out, n_mean, n_ctr, n_bias = (sem(n) for n in (
            "n_sq", "n_stat", "n_rstd", "n_out", "n_mean", "n_ctr", "n_bias"))
        norm_index = {}
        norms = [("ffn1", "rms", "ffn1_norm", None), ("mix", "rms", "mix_norm", None), ("ffn2", "rms", "ffn2_norm", None)]
        if stop != "block1":
            norms += [("ln_in", "ln", "ln_in_g", "ln_in_b"), ("ln1_0", "ln", "ln1_g0", "ln1_b0"),
                      ("ln2_0", "ln", "ln2_g0", "ln2_b0")]
        if full:
            norms += [("ln1_1", "ln", "ln1_g1", "ln1_b1")]
        for i, (name, kind, g, b) in enumerate(norms):
            ln_before = sum(1 for x in norms[:i] if x[1] == "ln")
            norm_index[name] = (i, ln_before, kind, g, b)
        splits = ["ffn1", "mix", "mixed0", "ffn2", "ln_in", "mixed1", "ln1_0", "ln2_0", "mixed2", "tok"]
        split_base = {s: 8 * i for i, s in enumerate(splits)}

        block = ctx.enter_context(nc.Block())

        def item_loop(eng, n0, count, step, peel_last=False, peel_first=False):
            pairs = count // 2
            lo = 1 if n0 == 0 or peel_first else 0
            hi = pairs - 1 if peel_last else pairs
            for j in range(2 * lo):
                step(n0 + j, (n0 + j) % 2, (n0 + j) // 2, j)
            if hi > lo:
                with eng.Fori(lo, hi) as i:
                    for b in range(2):
                        step(i * 2 + (n0 + b), (n0 + b) % 2, i + (n0 + b) // 2, i * 2 + b)
            for j in range(2 * hi, count):
                step(n0 + j, (n0 + j) % 2, (n0 + j) // 2, j)

        a_scores, a_max, a_exp, a_probs, a_turned, a_copied, a_pv = (sem(n) for n in (
            "a_scores", "a_max", "a_exp", "a_probs", "a_turned", "a_copied", "a_pv"))

        def chunk_ends(jobs):
            last = {}
            for x, job in enumerate(jobs):
                last[job["chunk"]] = 4 * x + 3
            return {u: c for c, u in last.items()}

        def pe_attention(pe, u0, jobs, base, extra=None):
            units = [(job, i) for job in jobs for i in range(NT)]

            def scores(x):
                (job, i), u = units[x], u0 + x
                if u >= 3:
                    pe.wait_ge(a_max, u - 2)
                w = (i + 1) * P
                nc.tensor.matmul(ps[:, u % 3, 0:w], job["q"][:, i * P:w], job["k"][:, 0:w],
                                 start=True, stop=True).then_inc(a_scores, 1)

            def turn(x):
                (job, i), u = units[x], u0 + x
                pe.wait_ge(a_probs, u + 1)
                if u >= 2:
                    pe.wait_ge(a_copied, u - 1)
                for j in range(i + 1):
                    mm = nc.tensor.transpose(ps[:, 3 + u % 2, j * P:(j + 1) * P],
                                             job["sc"][:, u % 3, j * P:(j + 1) * P], ident)
                mm.then_inc(a_turned, 1)

            def product(x):
                (job, i), u = units[x], u0 + x
                if extra:
                    extra(x)
                pe.wait_ge(a_copied, u + 1)
                c, h0 = job["chunk"], job["half"] * HD
                if job["start"] and i == 0 and c >= 2 and job["half"] == 0:
                    pe.wait_ge(x_lo, base + c - 1)
                for j in range(i + 1):
                    mm = nc.tensor.matmul(ps[h0:h0 + HD, 5 + c % 2, i * P:(i + 1) * P], job["v"](j),
                                          job["pt"][:, u % 3, j * P:(j + 1) * P],
                                          start=(job["start"] and i == 0 and j == 0),
                                          stop=(job["stop"] and i == NT - 1 and j == i))
                mm.then_inc(a_pv, 1)

            scores(0)
            scores(1)
            for x in range(len(units)):
                if x + 2 < len(units):
                    scores(x + 2)
                turn(x)
                if x >= 1:
                    product(x - 1)
            product(len(units) - 1)

        def act_attention(act, u0, jobs, base, extra=None):
            units = [(job, i) for job in jobs for i in range(NT)]
            ends = chunk_ends(jobs)

            def exp(x):
                (job, i), u = units[x], u0 + x
                act.wait_ge(a_max, u + 1)
                sc = job["sc"][:, u % 3, 0:(i + 1) * P]
                st = job["st"][:, u % 3]
                nc.scalar.activation(sc, sc, ACT.Exp, bias=st[:, 0:1], scale=-1.0,
                                     accum_out=st[:, 1:2]).then_inc(a_exp, 1)

            def copy(x):
                (job, i), u = units[x], u0 + x
                act.wait_ge(a_turned, u + 1)
                if u >= 3:
                    act.wait_ge(a_pv, u - 2)
                w = (i + 1) * P
                nc.scalar.copy(job["pt"][:, u % 3, 0:w], ps[:, 3 + u % 2, 0:w]).then_inc(a_copied, 1)

            def chunk_out(x):
                if x in ends:
                    c = ends[x]
                    act.wait_ge(a_pv, u0 + x + 1)
                    nc.scalar.copy(xh[:, c], ps[:, 5 + c % 2]).then_inc(x_hi, 1)

            exp(0)
            for x in range(len(units)):
                if x + 1 < len(units):
                    exp(x + 1)
                copy(x)
                if extra:
                    extra(x)
                chunk_out(x - 2)
            chunk_out(len(units) - 2)
            chunk_out(len(units) - 1)

        def dve_attention(dve, chain, u0, jobs, base):
            units = [(job, i) for job in jobs for i in range(NT)]
            ends = chunk_ends(jobs)

            def masked(x):
                (job, i), u = units[x], u0 + x
                w = (i + 1) * P
                dve.wait_ge(a_scores, u + 1)
                if u >= 3:
                    dve.wait_ge(a_turned, u - 2)
                lo = S - w
                nc.vector.tensor_tensor_reduce(job["sc"][:, u % 3, 0:w], ps[:, u % 3, 0:w], job["mask"][:, lo:lo + w],
                                               -SCALE, 3e38, ALU.add, ALU.min,
                                               job["st"][:, u % 3, 0:1]).then_inc(a_max, 1)

            def normalise(x):
                (job, i), u = units[x], u0 + x
                dve.wait_ge(a_exp, u + 1)
                st = job["st"][:, u % 3]
                chain.then(nc.vector.reciprocal(st[:, 2:3], st[:, 1:2]))
                sc = job["sc"][:, u % 3, 0:(i + 1) * P]
                if job["gate"] is None:
                    ins = nc.vector.tensor_scalar(sc, sc, st[:, 2:3], None, ALU.mult)
                else:
                    ins = nc.vector.tensor_scalar(sc, sc, st[:, 2:3], job["gate"](i), ALU.mult, ALU.mult)
                ins.then_inc(a_probs, 1)

            def chunk_out(x):
                if x in ends:
                    c = ends[x]
                    dve.wait_ge(x_hi, base + c + 1)
                    nc.vector.tensor_tensor(xl[:, c], ps[:, 5 + c % 2], xh[:, c].bitcast(F32),
                                            ALU.subtract).then_inc(x_lo, 1)

            masked(0)
            for x in range(len(units)):
                if x + 1 < len(units):
                    masked(x + 1)
                normalise(x)
                chunk_out(x - 3)
            for x in (3, 2, 1):
                chunk_out(len(units) - x)

        def jobs1():
            return [dict(chunk=h // 2, half=h % 2, start=True, stop=True, gate=None, mask=mask1, sc=sc1, pt=pt1, st=st1,
                         q=proj[(h % 2) * HD:(h % 2) * HD + HD, h // 2],
                         k=proj[(h % 2) * HD:(h % 2) * HD + HD, 4 + h // 2],
                         v=lambda j, h=h: vtok[:, h // 4, j, (h % 4) * HD:(h % 4 + 1) * HD])
                    for h in range(HEADS)]

        q_sq, q_stat, q_rstd, q_normed, q_turned, q_done = (sem(n) for n in (
            "q_sq", "q_stat", "q_rstd", "q_normed", "q_turned", "q_done"))
        tables1 = sem("tables1")
        g_act, g_dve = sem("g_act"), sem("g_dve")
        h_att, h_masked, h_turned, h_ktok, h_upd, h_state, h_out, h_sq, h_stat, h_rstd, h_rec = (sem(n) for n in (
            "h_att", "h_masked", "h_turned", "h_ktok", "h_upd", "h_state", "h_out", "h_sq", "h_stat", "h_rstd", "h_rec"))
        MIX0 = split_base["mixed0"]
        MIXED_ORDER = (4, 5, 6, 7, 0, 1, 2, 3)
        hq, hf, hg = proj[:, 8:12], proj[:, 12:16], proj[:, 16:20]
        hk = raw[:, :, ITEM:ITEM + 2 * S]

        def paired(ap):
            return ap.rearrange("p (a b) s -> p a (b s)", a=2)


        def flat(ap):
            return ap.rearrange("p a s -> p (a s)")

        def pe_block1_mixer(pe):
            def stat(c):
                pe.wait_ge(q_sq, c + 1)
                if c >= 2:
                    pe.wait_ge(q_rstd, c - 1)
                nc.tensor.matmul(ps[:, c % 2], consts[:, ONES_H:ONES_H + P], rn[:, c % 2], start=True,
                                 stop=True).then_inc(q_stat, 1)

            def turn(c):
                pe.wait_ge(q_normed, c + 1)
                if c >= 2:
                    pe.wait_ge(q_done, c - 1)
                nc.tensor.matmul(ps[:, 2 + c % 2], consts[:, ROT:ROT + P], proj[:, c], start=True,
                                 stop=True).then_inc(q_turned, 1)

            pe.wait_ge(evac_done, first["out0"])
            for c in range(9):
                if c < 8:
                    stat(c)
                if c >= 1:
                    turn(c - 1)
            pe.wait_ge(q_done, 8)
            pe_attention(pe, 0, jobs1(), MIX0)

            def scores(h):
                if h >= 2:
                    pe.wait_ge(h_masked, h - 1)
                for b in range(NT):
                    mm = nc.tensor.matmul(ps[:, h % 2, b * P:(b + 1) * P], hf[:, h, b * P:(b + 1) * P],
                                          hq[:, h, b * P:(b + 1) * P], start=True, stop=True)
                mm.then_inc(h_att, 1)
                if h >= 2:
                    pe.wait_ge(h_rstd, h - 1)
                for b in range(NT):
                    mm = nc.tensor.transpose(ps[:, 2 + h % 2, b * P:(b + 1) * P], hk[:, h // 2, (h % 2) * S + b * P:(h % 2) * S + (b + 1) * P], ident)
                mm.then_inc(h_turned, 1)

            def updates(h):
                pe.wait_ge(h_ktok, h + 1)
                if h >= 1:
                    pe.wait_ge(h_state, h)
                for c in range(NCHUNK - 1):
                    rows = slice((c % 2) * CHUNK, (c % 2) * CHUNK + CHUNK)
                    mm = nc.tensor.matmul(ps[:, 4 + c % 2, (c // 2) * P:(c // 2 + 1) * P], ktok[rows, h % 2, c // 2],
                                          itok[rows, h // 2, c // 2, (h % 2) * P:(h % 2 + 1) * P], start=True, stop=True)
                mm.then_inc(h_upd, 1)

            def output(h):
                pe.wait_ge(h_masked, h + 1)
                pe.wait_ge(h_state, h + 1)
                if h >= 2:
                    pe.wait_ge(x_lo, MIX0 + 4 + h - 1)
                for b in range(NT):
                    nc.tensor.matmul(ps[:, 6 + h % 2, b * P:(b + 1) * P], itok[:, h // 2, b, (h % 2) * P:(h % 2 + 1) * P],
                                     att[:, h % 2, b], start=(b == 0), stop=False)
                for c in range(1, NCHUNK):
                    mm = nc.tensor.matmul(ps[:, 6 + h % 2, c * CHUNK:(c + 1) * CHUNK], states[:, c - 1],
                                          hq[:, h, c * CHUNK:(c + 1) * CHUNK], start=False, stop=(c == NCHUNK - 1))
                mm.then_inc(h_out, 1)

            pe.wait_ge(x_lo, MIX0 + 4)
            pe.wait_ge(g_dve, 8)
            scores(0)
            updates(0)
            for h in range(4):
                if h < 3:
                    scores(h + 1)
                output(h)
                if h < 3:
                    updates(h + 1)
                pe.wait_ge(h_sq, h + 1)
                nc.tensor.matmul(ps[:, 2 + h % 2], consts[:, ONES_D:ONES_D + P], hn[:, 0], start=True,
                                 stop=True).then_inc(h_stat, 1)

        def act_gates(act, j):
            if j == 0:
                act.wait_ge(evac_done, first["tok0"])
                act.wait_ge(g_dve, 1)
                nc.scalar.activation(lbv[:, 1:3], lbv[:, 1:3], ACT.Exp).then_inc(g_act, 1)
                nc.scalar.activation(flat(hf), flat(hf), ACT.Sigmoid).then_inc(g_act, 1)
                nc.scalar.activation(flat(hg), flat(hg), ACT.Silu).then_inc(g_act, 1)
                act.preload_act_table_set(LN_EXP)
            if j == 1:
                act.wait_ge(g_dve, 3)
                nc.scalar.activation(flat(hf), flat(hf), ACT.Ln).then_inc(g_act, 1)
                act.wait_ge(g_dve, 4)
                nc.scalar.activation(hE[:], hG[:], ACT.Exp).then_inc(g_act, 1)
            if j == 2:
                act.wait_ge(g_dve, 5)
                nc.scalar.activation(hE[:], hG[:], ACT.Exp, scale=-1.0).then_inc(g_act, 1)
            if j == 3:
                act.wait_ge(g_dve, 7)
                nc.scalar.activation(hE[:], hE[:], ACT.Exp).then_inc(g_act, 1)

        def dve_gates(dve, chain, j):
            if j == 0:
                lb = vec("lb_logits")
                chain.then(nc.vector.tensor_tensor(lbv[:, 0], lb[:, 0:4], lb[:, 4:8], ALU.max))
                chain.then(nc.vector.tensor_tensor(lbv[:, 1], lb[:, 0:4], lbv[:, 0], ALU.subtract))
                nc.vector.tensor_tensor(lbv[:, 2], lb[:, 4:8], lbv[:, 0], ALU.subtract).then_inc(g_dve, 1)
                dve.wait_ge(g_act, 1)
                chain.then(nc.vector.tensor_tensor(lbv[:, 3], lbv[:, 1], lbv[:, 2], ALU.add))
                chain.then(nc.vector.reciprocal(lbv[:, 4], lbv[:, 3]))
                chain.then(nc.vector.tensor_tensor(lbv[:, 5], lbv[:, 1], lbv[:, 4], ALU.mult))
                chain.then(nc.vector.tensor_scalar(lbv[:, 6], lbv[:, 5], -1.0, 1.0, ALU.mult, ALU.add))
                dve.wait_ge(g_act, 2)
                for h in range(4):
                    ins = nc.vector.tensor_scalar(hf[:, h], hf[:, h], lbv[:, 6, h:h + 1], lbv[:, 5, h:h + 1], ALU.mult, ALU.add)
                ins.then_inc(g_dve, 1)
                dve.wait_ge(g_dve, 2)
                nc.vector.tensor_scalar(hk, paired(hf), -1.0, 1.0, ALU.mult, ALU.add).then_inc(g_dve, 1)
            if j == 1:
                dve.wait_ge(tables1, 48)
                dve.wait_ge(g_act, 4)
                for h in range(4):
                    ins = nc.vector.tensor_tensor_scan(hG[:, h // 2, (h % 2) * S:(h % 2 + 1) * S], reset[:], hf[:, h], 0.0, ALU.mult, ALU.add)
                ins.then_inc(g_dve, 1)
                dve.wait_ge(g_act, 5)
                chain.then(nc.vector.tensor_copy(paired(decay[:]), hE[:, :, CHUNK - 1::CHUNK]))
                nc.vector.tensor_tensor(paired(hq), paired(hq), hE[:], ALU.mult).then_inc(g_dve, 1)
            if j == 2:
                dve.wait_ge(g_act, 6)
                nc.vector.tensor_tensor(paired(hf), hk, hE[:], ALU.mult).then_inc(g_dve, 1)
                dve.wait_ge(g_dve, 6)
                gc, to = (ap.rearrange("p a (c s) -> p a c s", s=CHUNK) for ap in (hG, hE))
                nc.vector.tensor_tensor(to, gc[:, :, :, CHUNK - 1:CHUNK].to_broadcast([P, 2, 2 * NCHUNK, CHUNK]), gc,
                                        ALU.subtract).then_inc(g_dve, 1)
            if j == 3:
                dve.wait_ge(g_act, 7)
                nc.vector.tensor_tensor(hk, hk, hE[:], ALU.mult).then_inc(g_dve, 1)
                dve.wait_ge(g_dve, 8)

        def act_block1_mixer(act, chain):
            def square(c):
                if c >= 2:
                    act.wait_ge(q_normed, c - 1)
                nc.scalar.activation(rn[:, c % 2], proj[:, c], ACT.Square).then_inc(q_sq, 1)

            def rms(c):
                act.wait_ge(q_stat, c + 1)
                chain.then(nc.scalar.activation(rn[:, c % 2], ps[:, c % 2], ACT.Ln, bias=EPS))
                nc.scalar.activation(rn[:, c % 2], rn[:, c % 2], ACT.Exp, scale=-0.5).then_inc(q_rstd, 1)

            act.wait_ge(evac_done, first["out0"])
            act.wait_ge(g_dve, 8)
            act.preload_act_table_set(LN_EXP)
            square(0)
            for c in range(8):
                if c < 7:
                    square(c + 1)
                rms(c)
            act_attention(act, 0, jobs1(), MIX0)

            def keys(h):
                act.wait_ge(h_turned, h + 1)
                if h >= 2:
                    act.wait_ge(h_upd, h - 1)
                nc.scalar.copy(flat(ktok[:, h % 2]), ps[:, 2 + h % 2]).then_inc(h_ktok, 1)

            keys(0)
            for h in range(4):
                if h < 3:
                    keys(h + 1)
                act.wait_ge(h_out, h + 1)
                if h >= 1:
                    act.wait_ge(h_stat, h)
                nc.scalar.activation(hn[:, 0], ps[:, 6 + h % 2], ACT.Square).then_inc(h_sq, 1)
                act.wait_ge(h_stat, h + 1)
                chain.then(nc.scalar.activation(hn[:, 1], ps[:, 2 + h % 2], ACT.Ln, scale=float(KD), bias=EPS))
                nc.scalar.activation(hn[:, 1], hn[:, 1], ACT.Exp, scale=-0.5).then_inc(h_rstd, 1)
                act.wait_ge(h_rec, h + 1)
                nc.scalar.copy(xh[:, 4 + h], hn[:, 2]).then_inc(x_hi, 1)

        def dve_block1_mixer(dve, chain):
            def scale(c):
                dve.wait_ge(q_rstd, c + 1)
                w = vec("q_norm" if c < 4 else "k_norm")
                nc.vector.scalar_tensor_tensor(proj[:, c], proj[:, c], w, rn[:, c % 2], ALU.mult,
                                               ALU.mult).then_inc(q_normed, 1)

            def turn(c):
                dve.wait_ge(q_turned, c + 1)
                chain.then(nc.vector.tensor_tensor(proj[:, c], proj[:, c], rope[:, 0], ALU.mult))
                if c >= 1:
                    dve.wait_ge(q_done, c)
                chain.then(nc.vector.tensor_tensor(sc1[:, 0], ps[:, 2 + c % 2], rope[:, 1], ALU.mult))
                nc.vector.tensor_tensor(proj[:, c], proj[:, c], sc1[:, 0], ALU.add).then_inc(q_done, 1)

            dve.wait_ge(tables1, 48)
            for c in range(9):
                if c < 8:
                    scale(c)
                if c >= 1:
                    turn(c - 1)
            dve.wait_ge(q_done, 8)
            dve_attention(dve, chain, 0, jobs1(), MIX0)

            chain.then(nc.vector.memset(att[:], 0.0))
            hmask = consts[:, HMASK:HMASK + P].bitcast(I32)

            def masked(h):
                dve.wait_ge(h_att, h + 1)
                if h >= 2:
                    dve.wait_ge(h_out, h - 1)
                for b in range(NT):
                    ins = nc.vector.copy_predicated(att[:, h % 2, b], hmask, ps[:, h % 2, b * P:(b + 1) * P])
                ins.then_inc(h_masked, 1)

            def scan_states(h):
                dve.wait_ge(h_upd, h + 1)
                if h >= 1:
                    dve.wait_ge(h_out, h)
                chain.then(nc.vector.tensor_copy(states[:, 0], ps[:, 4, 0:P]))
                for c in range(1, NCHUNK - 1):
                    ins = nc.vector.scalar_tensor_tensor(states[:, c], states[:, c - 1], decay[:, h, c:c + 1],
                                                         ps[:, 4 + c % 2, (c // 2) * P:(c // 2 + 1) * P], ALU.mult, ALU.add)
                    if c < NCHUNK - 2:
                        chain.then(ins)
                ins.then_inc(h_state, 1)

            def finish(h):
                dve.wait_ge(h_rstd, h + 1)
                if h >= 1:
                    dve.wait_ge(x_lo, MIX0 + 4 + h)
                chain.then(nc.vector.scalar_tensor_tensor(hn[:, 2], ps[:, 6 + h % 2], vec("hg_out_norm"), hn[:, 1],
                                                          ALU.mult, ALU.mult))
                nc.vector.tensor_tensor(hn[:, 2], hn[:, 2], hg[:, h], ALU.mult).then_inc(h_rec, 1)
                dve.wait_ge(x_hi, MIX0 + 4 + h + 1)
                nc.vector.tensor_tensor(xl[:, 4 + h], hn[:, 2], xh[:, 4 + h].bitcast(F32), ALU.subtract).then_inc(x_lo, 1)

            masked(0)
            scan_states(0)
            for h in range(4):
                if h < 3:
                    masked(h + 1)
                finish(h)
                if h < 3:
                    scan_states(h + 1)

        d_dup, d_kdup, d_window, d_hi, d_lo = (sem(n) for n in ("d_dup", "d_kdup", "d_window", "d_hi", "d_lo"))
        d_hidden, d_gelu, d_small, d_keys = (sem(n) for n in ("d_hidden", "d_gelu", "d_small", "d_keys"))
        c_scores, c_shifted, c_exp, c_probs, c_turned, c_copied = (sem(n) for n in (
            "c_scores", "c_shifted", "c_exp", "c_probs", "c_turned", "c_copied"))
        v_conv, gates_ready, tables2 = sem("v_conv"), sem("gates_ready"), sem("tables2")
        w2k = cmpw[:, 0:256].rearrange("p (h m) -> p h m", h=2)
        w2v = cmpw[:, 256:384].rearrange("p (h m) -> p h m", h=2)
        b2v = cmpw[0:NCMP, 384:448]
        pos = cmpw[:, 448:480].rearrange("p (v c) -> p v c", v=2)
        UNITS1 = 4 * HEADS
        UNITS2 = 8 * HEADS

        def jobs2():
            return [dict(chunk=h // 2, half=h % 2, start=False, stop=(b == 1), mask=mask2, sc=sc2, pt=pt2, st=st2,
                         gate=lambda i, h=h, b=b: vgate[:, i, 256 + 8 * (b + 1) + h:257 + 8 * (b + 1) + h],
                         q=proj[(h % 2) * HD:(h % 2) * HD + HD, h // 2],
                         k=kdup[(h % 2) * HD:(h % 2) * HD + HD, 2 * b + h // 4],
                         v=lambda j, h=h, b=b: vgate[:, j, 128 * b + (h // 4) * HD:128 * b + (h // 4 + 1) * HD])
                    for h in range(HEADS) for b in range(2)]

        def turn_before(x):
            return (x + 4) // 8 if x % 8 == 4 and x + 4 < UNITS2 else None

        def windows(kv):
            return win[:, kv, 0:16 * WIN].rearrange("p (c a n) -> p c a n", c=16, a=2)

        def pe_mixer(pe, l):
            base = split_base[f"mixed{l + 1}"]
            n0 = first[f"cmp{l + 1}"]
            pe.wait_ge(evac_done, n0)
            for i, chunk in enumerate((4, 5, 6, 7)):
                for g, at in enumerate((SEL0, SEL1)):
                    mm = nc.tensor.matmul(ps[:, 2 * i + g], consts[:, at:at + P], proj[:, chunk], start=True, stop=True)
                if i % 2:
                    mm.then_inc(d_dup, 1)
            acc = 4 * (n0 % 2)
            for j in range(4):
                n, kv = n0 + j, j // 2
                slot = n % 2
                pe.wait_ge(d_lo, 2 * l + kv + 1)
                pe.wait_ge(d_window, 2 * l + 2)
                pe.wait_ge(d_kdup, l + 1)
                pe.wait_ge(lo_ready, n + 1)
                for hh in range(2):
                    for c in range(8):
                        cols = slice(c * 256 + hh * P, c * 256 + hh * P + P)
                        at = (8 * (j % 2) + c) * WIN
                        x2 = win[:, kv, at:at + WIDE]
                        dst = ps[:, acc + 2 * kv + hh, 0:WIDE]
                        nc.tensor.matmul(dst, wh[:, slot, cols], x2, start=(j % 2 == 0 and c == 0), stop=False)
                        mm = nc.tensor.matmul(dst, wl[:, slot, cols], x2, start=False, stop=(j % 2 == 1 and c == 7))
                mm.then_inc(item_done, 1)
            other = 4 - acc
            pe.wait_ge(d_gelu, 2 * l + 2)
            for hh in range(2):
                mm = nc.tensor.matmul(ps[:, other, 0:2 * NCMP], w2k[:, hh], hid[:, 0, hh], start=(hh == 0), stop=(hh == 1))
            for g in range(2):
                for hh in range(2):
                    mm = nc.tensor.matmul(ps[0:NCMP, other + 1 + g, 0:HD], hid[:, 1, hh, g * NCMP:(g + 1) * NCMP], w2v[:, hh],
                                          start=(hh == 0), stop=(hh == 1))
            mm.then_inc(d_small, 1)

            pe.wait_ge(d_keys, l + 1)
            for g in range(2):
                for r in range(2):
                    half = slice(r * HD, r * HD + HD)
                    for hh in range(2):
                        for i in range(NT):
                            at = (hh * NT + i) * NCMP
                            mm = nc.tensor.matmul(ps[:, 2 * g + r, at:at + NCMP], proj[half, 2 * g + hh, i * P:(i + 1) * P],
                                                  kcT[half, g * NCMP:(g + 1) * NCMP], start=True, stop=True)
                mm.then_inc(c_scores, 1)

            def turn_cmp(h):
                g, r, hh = h // 4, h % 2, (h % 4) // 2
                pe.wait_ge(c_probs, 2 * l + g + 1)
                pe.wait_ge(c_copied, HEADS * l + h) if HEADS * l + h else None
                for i in range(NT):
                    mm = nc.tensor.transpose(ps[0:NCMP, 7, i * P:(i + 1) * P], cs[:, g, r, hh, i], ident)
                mm.then_inc(c_turned, 1)

            def cmp_product(x):
                if x % 8 == 0:
                    h = x // 8
                    pe.wait_ge(c_copied, HEADS * l + h + 1)
                    if h % 2 == 0 and h >= 4:
                        pe.wait_ge(x_lo, base + 4 + h // 2 - 1)
                    r = (h % 2) * HD
                    nc.tensor.matmul(ps[r:r + HD, 5 + (h // 2) % 2], vcT[0:NCMP, h // 4], ptc[0:NCMP, h % 2],
                                     start=True, stop=False)
                if turn_before(x) is not None:
                    turn_cmp(turn_before(x))

            pe.wait_ge(c_shifted, 2 * l + 2)
            turn_cmp(0)
            pe_attention(pe, UNITS1 + UNITS2 * l, jobs2(), base + 4, cmp_product)

        def act_mixer(act, chain, l):
            base = split_base[f"mixed{l + 1}"]
            n0 = first[f"cmp{l + 1}"]
            ahead(act_split, n0 - 1, (n0 - 1) % 2, (n0 - 1) // 2, KD * 280, 0, 1)
            act.wait_ge(evac_done, n0)
            gates = vgate[:, :, 256:280]
            nc.scalar.activation(gates, gates, ACT.Sigmoid).then_inc(gates_ready, 1)
            act.wait_ge(d_dup, 2 * l + 2)
            nc.scalar.copy(flat(kdup), flat(ps[:, 4:8])).then_inc(d_kdup, 1)
            for kv in range(2):
                act.wait_ge(d_window, 2 * l + kv + 1)
                nc.scalar.copy(windows(kv)[:, :, 0], wnf.rearrange("p c g n -> p c (g n)")).then_inc(d_hi, 1)
            for j in range(4):
                n = n0 + j
                ahead(act_split, n, n % 2, n // 2, ITEM, j, 4)
                if j == 3:
                    act.wait_ge(v_conv, l + 1)
                    for c in range(4):
                        nc.scalar.copy(xh[:, 4 + c], proj[:, 12 + c]).then_inc(x_hi, 1)
                if j % 2:
                    act.wait_ge(d_hidden, 2 * l + j // 2 + 1)
                    h2 = hid[:, j // 2].rearrange("p h n -> p (h n)")
                    nc.scalar.activation(h2, h2, ACT.Gelu_apprx_tanh).then_inc(d_gelu, 1)
            for g in range(2):
                act.wait_ge(c_shifted, 2 * l + g + 1)
                nc.scalar.activation(cs_flat(g), cs_flat(g), ACT.Exp, scale=SCALE).then_inc(c_exp, 1)
            def copy_cmp(h):
                act.wait_ge(c_turned, HEADS * l + h + 1)
                if h >= 2:
                    act.wait_ge(a_pv, UNITS1 + UNITS2 * l + 8 * (h - 2) + 1)
                nc.scalar.copy(ptc[0:NCMP, h % 2], ps[0:NCMP, 7]).then_inc(c_copied, 1)

            copy_cmp(0)
            act_attention(act, UNITS1 + UNITS2 * l, jobs2(), base + 4,
                          lambda x: copy_cmp(turn_before(x - 1)) if turn_before(x - 1) is not None else None)

        def dve_convolution(dve, chain, l, j):
            u, bg, cg = proj[:, 8:12], proj[:, 12:16], proj[:, 16:20]
            w = vec(f"conv{l}")
            if j == 0:
                chain.then(nc.vector.tensor_tensor(flat(u), flat(u), flat(cg), ALU.mult))
                for c in range(4):
                    ins = nc.vector.tensor_scalar(cg[:, c], u[:, c], w[:, 8 + c:9 + c], None, ALU.mult)
                chain.then(ins)
            if j == 1:
                for back in (1, 2):
                    for c in range(4):
                        at = 4 * (2 - back) + c
                        ins = nc.vector.scalar_tensor_tensor(cg[:, c, back:S], u[:, c, 0:S - back], w[:, at:at + 1],
                                                             cg[:, c, back:S], ALU.mult, ALU.add)
                    chain.then(ins)
            if j == 2:
                nc.vector.tensor_tensor(flat(bg), flat(bg), flat(cg), ALU.mult).then_inc(v_conv, 1)
            if j == 3:
                base = split_base[f"mixed{l + 1}"]
                for c in range(4):
                    dve.wait_ge(x_hi, base + c + 1)
                    nc.vector.tensor_tensor(xl[:, 4 + c], bg[:, c], xh[:, 4 + c].bitcast(F32), ALU.subtract).then_inc(x_lo, 1)

        def dve_mixer(dve, chain, l):
            base = split_base[f"mixed{l + 1}"]
            n0 = first[f"cmp{l + 1}"]
            n = n0 - 1
            ahead(dve_split, n, n % 2, n // 2, KD * 280, 0, 1)
            dve.wait_ge(item_done, n + 1)
            nc.vector.tensor_copy(vgate[:], ps[:, 4 * (n % 2):4 * (n % 2) + 4, 0:280]).then_inc(evac_done, 1)

            dve.wait_ge(tables2, 48 * (l + 1))
            nc.vector.memset(win[:, :, 16 * WIN:].bitcast(F32), 0.0)
            dve.wait_ge(d_dup, 2 * l + 1)
            for kv in range(2):
                if kv:
                    dve.wait_ge(d_hi, 2 * l + 1)
                    dve.wait_ge(d_lo, 2 * l + 1)
                for g in range(2):
                    for par in range(2):
                        rows = slice(par * HD, par * HD + HD)
                        src = ps[rows, 2 * kv + g].rearrange("p (m c r) -> p c m r", c=8, r=2)
                        for ch in range(2):
                            ins = nc.vector.tensor_tensor(
                                wnf[rows, 8 * ch:8 * ch + 8, g], src[:, :, ch:ch + NCMP, par],
                                pos[rows, kv, 8 * ch:8 * ch + 8].unsqueeze(2).to_broadcast([HD, 8, NCMP]), ALU.add)
                ins.then_inc(d_window, 1)
                dve.wait_ge(d_hi, 2 * l + kv + 1)
                dve.wait_ge(d_window, 2 * l + kv + 1)
                hi, lo = windows(kv)[:, :, 0], windows(kv)[:, :, 1]
                nc.vector.tensor_tensor(lo, wnf.rearrange("p c g n -> p c (g n)"), hi.bitcast(F32),
                                        ALU.subtract).then_inc(d_lo, 1)
            acc = 4 * (n0 % 2)
            for j in range(4):
                n, kv = n0 + j, j // 2
                ahead(dve_split, n, n % 2, n // 2, ITEM, j, 4)
                dve_convolution(dve, chain, l, j)
                dve.wait_ge(item_done, n + 1)
                if j % 2 == 0:
                    dve.sem_inc(evac_done, 1)
                    continue
                for hh in range(2):
                    b1 = vec(f"cmp_b1{l}")[:, 2 * kv + hh:2 * kv + hh + 1]
                    ins = nc.vector.tensor_scalar(hid[:, kv, hh], ps[:, acc + 2 * kv + hh, 0:2 * NCMP], b1, None, ALU.add)
                chain.then(ins)
                for hh in range(2):
                    ins = nc.vector.tensor_tensor(hid[:, kv, hh], hid[:, kv, hh],
                                                  ps[:, acc + 2 * kv + hh, 2 * NCMP:4 * NCMP], ALU.add)
                ins.then_inc(evac_done, 1)
                dve.wait_ge(evac_done, n + 1)
                dve.sem_inc(d_hidden, 1)
            other = 4 - acc
            dve.wait_ge(d_small, l + 1)
            nc.vector.tensor_scalar(kcT[:], ps[:, other, 0:2 * NCMP], vec(f"cmp_b2k{l}"), None, ALU.add)
            for g in range(2):
                ins = nc.vector.tensor_tensor(vcT[0:NCMP, g], ps[0:NCMP, other + 1 + g, 0:HD], b2v, ALU.add)
            ins.then_inc(d_keys, 1)

            for g in range(2):
                dve.wait_ge(c_scores, 2 * l + g + 1)
                for r in range(2):
                    ins = nc.vector.tensor_tensor(cs[:, g, r].rearrange("p h i n -> p h (i n)"),
                                                  ps[:, 2 * g + r, 0:2 * NT * NCMP].rearrange("p (h n) -> p h n", h=2),
                                                  cmask[:, 0:1].to_broadcast([P, 2, NT * NCMP]), ALU.add)
                chain.then(ins)
                rows16 = cs_flat(g).rearrange("p (a n) -> p a n", n=NCMP)
                chain.then(nc.vector.tensor_reduce(cst[:, g, 0], rows16, AX.X, ALU.max))
                nc.vector.tensor_tensor(rows16, rows16, cst[:, g, 0].unsqueeze(2).to_broadcast([P, 16, NCMP]),
                                        ALU.subtract).then_inc(c_shifted, 1)
            dve.wait_ge(gates_ready, l + 1)
            for g in range(2):
                dve.wait_ge(c_exp, 2 * l + g + 1)
                rows16 = cs_flat(g).rearrange("p (a n) -> p a n", n=NCMP)
                chain.then(nc.vector.tensor_reduce(cst[:, g, 1], rows16, AX.X, ALU.add))
                chain.then(nc.vector.reciprocal(cst[:, g, 2], cst[:, g, 1]))
                w = cst[:, g, 2].rearrange("p (r h i) -> p r h i", r=2, h=2)
                gate = vgate[:, :, 256 + 4 * g:260 + 4 * g].rearrange("p i (h r) -> p r h i", r=2)
                for r in range(2):
                    ins = nc.vector.tensor_tensor(w[:, r], w[:, r], gate[:, r], ALU.mult)
                chain.then(ins)
                rows4 = cs_flat(g).rearrange("p (a n) -> p a n", n=NT * NCMP)
                chain.then(nc.vector.tensor_tensor(rows4, rows4, cmask[:, 1:2].to_broadcast([P, 4, NT * NCMP]), ALU.mult))
                nc.vector.tensor_tensor(rows16, rows16, cst[:, g, 2].unsqueeze(2).to_broadcast([P, 16, NCMP]),
                                        ALU.mult).then_inc(c_probs, 1)

            dve_attention(dve, chain, UNITS1 + UNITS2 * l, jobs2(), base + 4)

        def cs_flat(g):
            return cs[:, g].rearrange("p r h i n -> p (r h i n)")

        m_turned, m_hi, m_lo, m_logits, m_pair, m_pair_exp, m_picked, m_ranks, m_list = (sem(n) for n in (
            "m_turned", "m_hi", "m_lo", "m_logits", "m_pair", "m_pair_exp", "m_picked", "m_ranks", "m_list"))
        tables3 = sem("tables3")
        e_raw = [sem(f"e_raw{i}") for i in range(4)]
        e_hi, e_lo, e_sel, e_pick, e_pickT, e_pickT_out, e_gate, e_gate_out, e_gath, e_gath_out = (sem(n) for n in (
            "e_hi", "e_lo", "e_sel", "e_pick", "e_pickT", "e_pickT_out", "e_gate", "e_gate_out", "e_gath", "e_gath_out"))
        e_done, e_part, e_sum, e_silu, e_glu, e_glu_hi, e_glu_lo, e_y_hi, e_y_lo, e_back, e_acc, e_y_turned = (sem(n) for n in (
            "e_done", "e_part", "e_sum", "e_silu", "e_glu", "e_glu_hi", "e_glu_lo", "e_y_hi", "e_y_lo", "e_back", "e_acc",
            "e_y_turned"))
        lastrow_loaded = sem("lastrow_loaded")
        lastrow = raw_m[:, 3, 0:2 * D].rearrange("p (r d) -> p r d", r=2)
        f_stat, f_rstd, f_row = sem("f_stat"), sem("f_rstd"), sem("f_row")
        NP_AT = PLAN - 1
        xh_tok = xh.rearrange("p k s -> p (k s)").rearrange("p (t d) -> p t d", t=NT)
        xl_tok = xl.rearrange("p k s -> p (k s)").rearrange("p (t d) -> p t d", t=NT)
        iota, upper, ones = mtab[:, 0:WIDE], mtab[:, WIDE:WIDE + P], mtab[:, WIDE + P:WIDE + 2 * P]
        iota8 = mtab[:, WIDE + 2 * P:WIDE + 2 * P + NE]
        router = mtab[:, WIDE + 2 * P + NE:WIDE + 2 * P + NE + KD * NE].rearrange("p (k e) -> p k e", e=NE)
        def moe_size(n):
            n %= NI
            return ITEM if n < FE else DOWN[n - FE][1] * FE * TILE

        def moe_slots(sl, n):
            return ps[:, 2 * (n % 2):2 * (n % 2) + 2, sl]

        def sp_moe(sp):
            def load(expert, n):
                if n < FE:
                    src = t["moe_up"][bass.ds(expert * FE + n, 1) if not isinstance(expert, int) else slice(n, n + 1)]
                    sp.dma_start(raw_m[:, n % 4, 0:ITEM], src.rearrange("o p c -> (o p) c")).then_inc(e_raw[n % 4], 16)
                else:
                    m, w = DOWN[n - FE]
                    src = t["moe_down"][bass.ds(expert * KD + m, w) if not isinstance(expert, int) else slice(m, m + w)]
                    dst = raw_m[:, n % 4, 0:w * FE * TILE].rearrange("p (o c) -> p o c", o=w)
                    sp.dma_start(dst, src.rearrange("o p c -> p o c")).then_inc(e_raw[n % 4], 16)

            sp.wait_ge(evac_done, len(sizes))
            for n in range(NI):
                if n >= 4:
                    sp.wait_ge(e_lo, 2 * (n - 3))
                load(0, n)
            sp.wait_ge(m_list, 1)
            passes = sp.value_load(plan[0:1, 0, NP_AT:NP_AT + 1], min_val=NE, max_val=NE + EXTRA)
            with sp.Fori(0, passes - 1) as q:
                expert = sp.value_load(plan[0:1, 1, bass.ds(q + 1, 1)], min_val=0, max_val=NE - 1)
                for n in range(NI):
                    sp.wait_ge(e_lo, q * (2 * NI) + 2 * (NI + n - 3))
                    load(expert, n)
            for n in range(2):
                sp.wait_ge(e_lo, passes * (2 * NI))
                load(0, n)
            sp.dma_start(raw_m[:, 3, 0:2 * D], t["lastrow"].to_broadcast([P, 2 * D])).then_inc(lastrow_loaded, 16)
            for tt in range(NT):
                sp.wait_ge(f_row, tt + 1)
                sp.dma_start(out[tt * P:(tt + 1) * P], acc[:, tt]).then_inc(stored, 16)
            sp.wait_ge(stored, 16 * NT)

        def pe_moe(pe):
            pe.wait_ge(n_bias, KD)
            for b in range(8):
                tt, kh = b // 2, b % 2
                if b >= 4:
                    pe.wait_ge(m_lo, b - 3)
                for kk in range(4):
                    mm = nc.tensor.transpose(ps[:, b % 4, kk * P:(kk + 1) * P], xT[:, 4 * kh + kk, tt * P:(tt + 1) * P], ident)
                mm.then_inc(m_turned, 1)
            pe.wait_ge(tables3, 16)
            for tt in range(NT):
                for k in range(KD):
                    mm = nc.tensor.matmul(ps[:, 4, tt * NE:(tt + 1) * NE], xT[:, k, tt * P:(tt + 1) * P], router[:, k],
                                          start=(k == 0), stop=(k == KD - 1))
            mm.then_inc(m_logits, 1)
            pe.wait_ge(m_picked, 1)
            for tt in range(NT + 1):
                for s in range(tt + 1 if tt < NT else NT):
                    mm = nc.tensor.matmul(ps[:, 5, tt * NE:(tt + 1) * NE], upper if s == tt else ones, picked[:, s],
                                          start=(s == 0), stop=(s == min(tt, NT - 1)))
            mm.then_inc(m_ranks, 1)

            pe.wait_ge(m_list, 1)
            passes = pe.value_load(plan[0:1, 0, NP_AT:NP_AT + 1], min_val=NE, max_val=NE + EXTRA)

            def gather(p):
                pe.wait_ge(e_pick, p + 1)
                for k in range(KD):
                    if k >= 4:
                        pe.wait_ge(e_gath_out, p * KD + (k - 3))
                    for part_no, src in enumerate((xh_tok, xl_tok)):
                        for tt in range(NT):
                            mm = nc.tensor.matmul(ps[:, 4 + k % 4, part_no * WIDE:(part_no + 1) * WIDE],
                                                  src[:, tt, k * P:(k + 1) * P], pick[:, tt], start=(tt == 0), stop=(tt == NT - 1))
                    mm.then_inc(e_gath, 1)

            def turn_y(p):
                pe.wait_ge(e_sum, p * NI + 2)
                for m in range(KD):
                    nc.tensor.transpose(ps[:, 4 + m // 4, (m % 4) * P:(m % 4 + 1) * P], yf[:, m, 0:P], ident)
                for m in range(KD):
                    mm = nc.tensor.transpose(ps[0:JT[1], 6 + m // 4, (m % 4) * P:(m % 4 + 1) * P], yf[:, m, P:CAP], ident)
                mm.then_inc(e_y_turned, 1)

            def scatter(p, groups):
                pe.wait_ge(e_y_lo, p * 2 + 2)
                for g in groups:
                    tt, half = g // 2, g % 2
                    if g >= 4:
                        pe.wait_ge(e_acc, p * 8 + (g - 3))
                    for jt, w in enumerate(JT):
                        turned = pickT[0:w, jt, tt * P:(tt + 1) * P]
                        nc.tensor.matmul(ps[:, 4 + g % 4], turned, yh[0:w, jt, half * S:(half + 1) * S], start=(jt == 0), stop=False)
                        mm = nc.tensor.matmul(ps[:, 4 + g % 4], turned, yl[0:w, jt, half * S:(half + 1) * S],
                                              start=False, stop=(jt == 1))
                    mm.then_inc(e_back, 1)

            gather(0)
            with pe.Fori(0, passes) as p:
                def item(n):
                    chunks, ops, width = (KD, xg, 2) if n < FE else (FE, gg, DOWN[n - FE][1])
                    pe.wait_ge(e_sum, p * NI + (n + 1))
                    for m in range(width):
                        if width == 2:
                            pe.wait_ge(e_lo, p * (2 * NI) + (2 * n + m + 1))
                        else:
                            pe.wait_ge(e_lo, p * (2 * NI) + (2 * n + 2))
                        bank = 2 * (n % 2) + m
                        for k in range(chunks):
                            cols = slice((m * chunks + k) * TILE, (m * chunks + k + 1) * TILE)
                            x2 = ops[:, k].rearrange("p a c -> p (a c)")
                            low = lambda: nc.tensor.matmul(ps[:, bank, 0:WIDE], wml[:, n % 2, cols], x2[:, 0:WIDE],
                                                           start=False, stop=False)
                            if k == chunks - 1:
                                low()
                            mm = nc.tensor.matmul(ps[:, bank, 0:2 * CAP], wmh[:, n % 2, cols], x2, start=(k == 0),
                                                  stop=(k == chunks - 1))
                            if k < chunks - 1:
                                low()
                    mm.then_inc(e_done, 1)

                pe.wait_ge(e_gath_out, p * KD + KD)
                item(0)
                item(1)
                turn_y(p)
                item(2)
                for n in range(3, 7):
                    item(n)
                    scatter(p, (2 * n - 6, 2 * n - 5))
                item(7)
                pe.wait_ge(e_acc, p * 8 + 8)
                for jt, w in enumerate(JT):
                    for tt in range(NT):
                        mm = nc.tensor.transpose(ps[0:w, 4 + jt, tt * P:(tt + 1) * P],
                                                 pick[:, tt, jt * P:jt * P + w].bitcast(F32), ident)
                mm.then_inc(e_pickT, 1)
                for jt, w in enumerate(JT):
                    for tt in range(NT):
                        mm = nc.tensor.matmul(ps[0:w, 6, jt:jt + 1], pick[:, tt, jt * P:jt * P + w].bitcast(F32),
                                              gate_col[:, tt:tt + 1], start=(tt == 0), stop=(tt == NT - 1))
                mm.then_inc(e_gate, 1)
                for n in range(8, FE):
                    item(n)
                pe.wait_ge(e_pickT_out, p + 1)
                pe.wait_ge(e_gate_out, p + 1)
                gather(p + 1)
                pe.wait_ge(e_glu_lo, p * FE + FE)
                for n in range(FE, NI):
                    item(n)
            pe.wait_ge(e_gath_out, passes * KD + KD)
            turn_y(passes)
            scatter(passes, range(8))

        def act_moe(act, chain):
            for b in range(8):
                tt, kh = b // 2, b % 2
                act.wait_ge(m_turned, b + 1)
                nc.scalar.copy(xh_tok[:, tt, kh * S:(kh + 1) * S], ps[:, b % 4]).then_inc(m_hi, 1)
            act.wait_ge(m_pair, 1)
            nc.scalar.activation(pair[:, 0], pair[:, 0], ACT.Exp).then_inc(m_pair_exp, 1)
            act.wait_ge(m_list, 1)
            passes = act.value_load(plan[0:1, 0, NP_AT:NP_AT + 1], min_val=NE, max_val=NE + EXTRA)

            def split(p, n):
                act.wait_ge(e_raw[n % 4], (p * (NI // 4) + (n // 4 + 1)) * 16)
                half = moe_size(n) // 2
                for h in range(2):
                    cols = slice(h * half, (h + 1) * half)
                    nc.scalar.copy(wmh[:, n % 2, cols], raw_m[:, n % 4, cols]).then_inc(e_hi, 1)

            def gathered(p):
                for k in range(KD):
                    act.wait_ge(e_gath, p * KD + (k + 1))
                    nc.scalar.copy(xg[:, k], ps[:, 4 + k % 4].rearrange("p (a c) -> p a c", a=2)[:, :, 0:CAP]).then_inc(e_gath_out, 1)

            def outputs_hi(p):
                act.wait_ge(e_y_turned, p + 1)
                for jt, w in enumerate(JT):
                    nc.scalar.activation(yh[0:w, jt], ps[0:w, 4 + 2 * jt:6 + 2 * jt].rearrange("p b s -> p (b s)"), ACT.Copy,
                                         scale=gate_row[0:w, jt:jt + 1]).then_inc(e_y_hi, 1)

            split(0, 0)
            split(0, 1)
            gathered(0)
            with act.Fori(0, passes) as p:
                for n in range(NI):
                    w = 2 if n < FE else DOWN[n - FE][1]
                    act.wait_ge(e_done, p * NI + n + 1)
                    act.wait_ge(e_sum, p * NI + n + 1)
                    nc.scalar.copy(part[:, n % 2, 0:w], moe_slots(slice(CAP, 2 * CAP), n)[:, 0:w]).then_inc(e_part, 1)
                    if n + 2 >= NI:
                        split(p + 1, n + 2 - NI)
                    elif n != FE - 1:
                        split(p, n + 2)
                    if n < FE:
                        act.wait_ge(e_sum, p * NI + n + 3)
                        nc.scalar.activation(glu_t[:, n % 2], both[:, n % 2, 0], ACT.Silu).then_inc(e_silu, 1)
                        act.wait_ge(e_glu, p * FE + n + 1)
                        nc.scalar.copy(gg[:, n, 0], glu[:, n % 2]).then_inc(e_glu_hi, 1)
                    if n == 1:
                        outputs_hi(p)
                    if n == 7:
                        act.wait_ge(e_pickT, p + 1)
                        nc.scalar.copy(pickT[:, 0], ps[:, 4])
                        nc.scalar.copy(pickT[0:JT[1], 1], ps[0:JT[1], 5]).then_inc(e_pickT_out, 1)
                    if n == FE - 1:
                        gathered(p + 1)
                        split(p, n + 2)
            outputs_hi(passes)
            act.preload_act_table_set(LN_EXP)
            for tt in range(NT):
                act.wait_ge(f_stat, tt + 1)
                chain.then(nc.scalar.activation(mv[:, tt, 2:3], mv[:, tt, 1:2], ACT.Ln, bias=LN_EPS))
                nc.scalar.activation(mv[:, tt, 3:4], mv[:, tt, 2:3], ACT.Exp, scale=-0.5).then_inc(f_rstd, 1)

        def dve_moe(dve, chain):
            for b in range(8):
                tt, kh = b // 2, b % 2
                cols = slice(kh * S, (kh + 1) * S)
                dve.wait_ge(m_hi, b + 1)
                nc.vector.tensor_tensor(xl_tok[:, tt, cols], ps[:, b % 4], xh_tok[:, tt, cols].bitcast(F32), ALU.subtract)
                nc.vector.tensor_scalar(acc[:, tt, cols], ps[:, b % 4], ALPHA, None, ALU.mult).then_inc(m_lo, 1)
            dve.wait_ge(m_logits, 1)
            chain.then(nc.vector.tensor_copy(rt[:, 0], ps[:, 4, 0:NT * NE]))
            lg, top = (rt[:, i].rearrange("p (t e) -> p t e", e=NE) for i in (0, 1))
            for tt in range(NT):
                ins = nc.vector.max(top[:, tt], lg[:, tt])
            chain.then(ins)
            for tt in range(NT):
                ins = nc.vector.max_index(top_at[:, tt], top[:, tt], lg[:, tt])
            chain.then(ins)
            chain.then(nc.vector.tensor_copy(rt[:, 2], top_at.rearrange("p t e -> p (t e)")))
            at = rt[:, 2].rearrange("p (t e) -> p t e", e=NE)
            nc.vector.tensor_tensor(pair[:, 0], top[:, :, 1], top[:, :, 0], ALU.subtract).then_inc(m_pair, 1)
            dve.wait_ge(m_pair_exp, 1)
            chain.then(nc.vector.tensor_scalar(pair[:, 1], pair[:, 0], 1.0, None, ALU.add))
            chain.then(nc.vector.reciprocal(pair[:, 2], pair[:, 1]))
            chain.then(nc.vector.tensor_tensor(pair[:, 3], pair[:, 0], pair[:, 2], ALU.mult))
            wide = [P, NT, NE]
            iota_b = iota8.unsqueeze(1).to_broadcast(wide)
            is1, is2 = (rt[:, i].rearrange("p (t e) -> p t e", e=NE) for i in (3, 4))
            nc.vector.tensor_tensor(is1, iota_b, at[:, :, 0:1].to_broadcast(wide), ALU.is_equal)
            chain.then(nc.vector.tensor_tensor(is2, iota_b, at[:, :, 1:2].to_broadcast(wide), ALU.is_equal))
            nc.vector.tensor_tensor(picked[:], is1, is2, ALU.add).then_inc(m_picked, 1)
            dve.wait_ge(m_picked, 1)
            nc.vector.tensor_tensor(is1, is1, pair[:, 2].unsqueeze(2).to_broadcast(wide), ALU.mult)
            chain.then(nc.vector.tensor_tensor(is2, is2, pair[:, 3].unsqueeze(2).to_broadcast(wide), ALU.mult))
            chain.then(nc.vector.tensor_tensor(gates.rearrange("p e t -> p t e"), is1, is2, ALU.add))
            dve.wait_ge(m_ranks, 1)
            chain.then(nc.vector.scalar_tensor_tensor(rt[:, 5], ps[:, 5, 0:NT * NE], 1.0,
                                                      picked.rearrange("p t e -> p (t e)"), ALU.add, ALU.mult))
            for r in range(BLOCKS):
                nc.vector.tensor_scalar(ranks[:, r * NE:(r + 1) * NE].rearrange("p e t -> p t e"),
                                        rt[:, 5].rearrange("p (t e) -> p t e", e=NE), -1.0 - r * CAP, None, ALU.add)
            chain.then(nc.vector.memset(plan_f[:], 0.0))
            for r in range(1, BLOCKS):
                nc.vector.tensor_scalar(over[:, 0, (r - 1) * NE:r * NE], ps[0:1, 5, NT * NE:(NT + 1) * NE], float(r * CAP),
                                        None, ALU.is_gt)
                nc.vector.tensor_copy(over[:, 3, (r - 1) * NE:r * NE], iota8[0:1])
            nc.vector.tensor_copy(plan_f[:, 0, 0:NE], iota8[0:1])
            chain.then(nc.vector.tensor_copy(plan_f[:, 1, 0:NE], iota8[0:1]))
            more = (BLOCKS - 1) * NE
            chain.then(nc.vector.tensor_tensor_scan(over[:, 1], ones[0:1, 0:more], over[:, 0], 0.0, ALU.mult, ALU.add))
            chain.then(nc.vector.tensor_tensor(over[:, 2], over[:, 0], over[:, 1], ALU.mult))
            wide = [1, EXTRA, more]
            turn = iota[0:1, 1:1 + EXTRA].unsqueeze(2).to_broadcast(wide)
            chain.then(nc.vector.tensor_tensor(match[:, 0], over[:, 2:3].to_broadcast(wide), turn, ALU.is_equal))
            for rowno, value in ((0, iota[0:1, NE:NE + more]), (1, over[:, 3])):
                chain.then(nc.vector.tensor_tensor(match[:, 1], match[:, 0], value.unsqueeze(1).to_broadcast(wide), ALU.mult))
                chain.then(nc.vector.tensor_reduce(plan_f[:, rowno, NE:NE + EXTRA], match[:, 1], AX.X, ALU.add))
            chain.then(nc.vector.tensor_scalar(plan_f[:, 0, NP_AT:NP_AT + 1], over[:, 1, more - 1:more], float(NE), None, ALU.add))
            nc.vector.memset(pickT[:].bitcast(F32), 0.0)
            nc.vector.memset(gate_row[:], 0.0)
            nc.vector.memset(yf[:], 0.0).then_inc(e_sum, 2)
            nc.vector.tensor_copy(plan[:], plan_f[:]).then_inc(m_list, 1)

            dve.wait_ge(m_list, 1)
            passes = dve.value_load(plan[0:1, 0, NP_AT:NP_AT + 1], min_val=NE, max_val=NE + EXTRA)

            def choose(p):
                row = dve.value_load(plan[0:1, 0, bass.ds(p, 1)], min_val=0, max_val=BLOCKS * NE - 1)
                expert = dve.value_load(plan[0:1, 1, bass.ds(p, 1)], min_val=0, max_val=NE - 1)
                nc.vector.tensor_copy(rank_col[:], ranks[:, bass.ds(row, 1)].rearrange("p o t -> p (o t)"))
                nc.vector.tensor_copy(gate_col[:], gates[:, bass.ds(expert, 1)].rearrange("p o t -> p (o t)")).then_inc(e_sel, 1)
                dve.wait_ge(e_sel, p + 1)
                for tt in range(NT):
                    ins = nc.vector.tensor_scalar(pick[:, tt], iota, rank_col[:, tt:tt + 1], None, ALU.is_equal)
                ins.then_inc(e_pick, 1)

            def split(p, n):
                half = moe_size(n) // 2
                for h in range(2):
                    cols = slice(h * half, (h + 1) * half)
                    dve.wait_ge(e_hi, p * (2 * NI) + (2 * n + h + 1))
                    nc.vector.tensor_tensor(wml[:, n % 2, cols], raw_m[:, n % 4, cols], wmh[:, n % 2, cols].bitcast(F32),
                                            ALU.subtract).then_inc(e_lo, 1)

            def scattered(p, groups):
                for g in groups:
                    tt, half = g // 2, g % 2
                    dve.wait_ge(e_back, p * 8 + (g + 1))
                    a = acc[:, tt, half * S:(half + 1) * S]
                    nc.vector.tensor_tensor(a, a, ps[:, 4 + g % 4], ALU.add).then_inc(e_acc, 1)

            def outputs_lo(p):
                for jt, w in enumerate(JT):
                    dve.wait_ge(e_y_hi, p * 2 + jt + 1)
                    nc.vector.scalar_tensor_tensor(yl[0:w, jt], ps[0:w, 4 + 2 * jt:6 + 2 * jt].rearrange("p b s -> p (b s)"),
                                                   gate_row[0:w, jt:jt + 1], yh[0:w, jt].bitcast(F32), ALU.mult,
                                                   ALU.subtract).then_inc(e_y_lo, 1)

            choose(0)
            split(0, 0)
            split(0, 1)
            with dve.Fori(0, passes) as p:
                for n in range(NI):
                    w = 2 if n < FE else DOWN[n - FE][1]
                    dst = both[:, n % 2] if n < FE else yf[:, DOWN[n - FE][0]:DOWN[n - FE][0] + w]
                    dve.wait_ge(e_part, p * NI + n + 1)
                    nc.vector.tensor_tensor(dst, moe_slots(slice(0, CAP), n)[:, 0:w], part[:, n % 2, 0:w], ALU.add).then_inc(e_sum, 1)
                    if n + 2 >= NI:
                        split(p + 1, n + 2 - NI)
                    elif n != FE - 1:
                        split(p, n + 2)
                    if n < FE:
                        dve.wait_ge(e_silu, p * FE + n + 1)
                        if n >= 2:
                            dve.wait_ge(e_glu_lo, p * FE + n - 1)
                        nc.vector.tensor_tensor(glu[:, n % 2], glu_t[:, n % 2], both[:, n % 2, 1], ALU.mult).then_inc(e_glu, 1)
                        dve.wait_ge(e_glu_hi, p * FE + n + 1)
                        nc.vector.tensor_tensor(gg[:, n, 1], glu[:, n % 2], gg[:, n, 0].bitcast(F32), ALU.subtract).then_inc(e_glu_lo, 1)
                    if n == 1:
                        outputs_lo(p)
                    if n == FE - 1:
                        split(p, n + 2)
                    if 3 <= n < 7:
                        scattered(p, (2 * n - 6, 2 * n - 5))
                    if n == 7:
                        dve.wait_ge(e_gate, p + 1)
                        nc.vector.tensor_copy(gate_row[:, 0:1], ps[:, 6, 0:1])
                        nc.vector.tensor_copy(gate_row[0:JT[1], 1:2], ps[0:JT[1], 6, 1:2]).then_inc(e_gate_out, 1)
                        dve.wait_ge(e_pick, p + 1)
                        choose(p + 1)
            outputs_lo(passes)

            def finish(tt):
                dve.wait_ge(f_rstd, tt + 1)
                chain.then(nc.vector.scalar_tensor_tensor(acc[:, tt], acc[:, tt], mv[:, tt, 0:1], lastrow[:, 0],
                                                          ALU.subtract, ALU.mult))
                nc.vector.scalar_tensor_tensor(acc[:, tt], acc[:, tt], mv[:, tt, 3:4], lastrow[:, 1],
                                               ALU.mult, ALU.add).then_inc(f_row, 1)

            dve.wait_ge(lastrow_loaded, 16)
            for tt in range(NT):
                scattered(passes, (2 * tt, 2 * tt + 1))
                dve.wait_ge(e_acc, passes * 8 + (2 * tt + 2))
                for half in range(2):
                    ins = nc.vector.bn_stats(bn[:, tt, half], acc[:, tt, half * S:(half + 1) * S])
                chain.then(ins)
                nc.vector.bn_aggr(mv[:, tt, 0:2], bn[:, tt].rearrange("p h s -> p (h s)")).then_inc(f_stat, 1)
                if tt >= 1:
                    finish(tt - 1)
            finish(NT - 1)

        @block.sync
        def _(sp):
            sp.dma_start(xT[:], t["xT"]).then_inc(x_loaded, 16)
            sp.dma_start(consts[:], t["consts"]).then_inc(consts_loaded, 16)
            sp.dma_start(vecs[:], t["vecs"]).then_inc(consts_loaded, 16)

            def load_items(n0, count, size, source):
                def step(n, slot, half, j):
                    if not (isinstance(n, int) and n < 2):
                        sp.wait_ge(lo_ready, n - 1)
                    at = source[j] if isinstance(j, int) else source[bass.ds(j, 1)].rearrange("o p c -> (o p) c")
                    sp.dma_start(raw[:, slot, 0:size], at).then_inc(raw_loaded[slot], 16)
                item_loop(sp, n0, count, step)

            def load_ffn(name):
                at = 0
                for part, n in enumerate(FF_PARTS):
                    load_items(first[f"{name}_up{part}"], n, ITEM, t[f"{name}_up"][at:at + n])
                    load_items(first[f"{name}_down{part}"], 4, 2 * n * TILE, t[f"{name}_down{part}"])
                    at += n

            load_ffn("ffn1")
            load_items(first["in0"], NQKV // 2, ITEM, t["in0"])
            load_items(first["tok0"], 4, ITEM, t["tok0"])
            load_items(first["out0"], 4, ITEM, t["out0"])
            load_ffn("ffn2")
            for l in range(0 if stop == "block1" else 1 if stop == "layer1" else 2):
                load_items(first[f"in{l + 1}"], NQKV // 2, ITEM, t[f"in{l + 1}"])
                load_items(first[f"tok{l + 1}"], 1, KD * 280, t[f"tok{l + 1}"])
                load_items(first[f"cmp{l + 1}"], 4, ITEM, t[f"cmp{l + 1}"])
                load_items(first[f"out{l + 1}"], 4, ITEM, t[f"out{l + 1}"])
                if l == 0:
                    load_ffn("ffn3")
            if full:
                sp_moe(sp)
            if not full:
                sp.wait_ge(evac_done, len(sizes))
                if stop == "layer1":
                    sp.wait_ge(x_lo, split_base["ln2_0"] + KD)
                sp.dma_start(out, xT[:]).then_inc(stored, 16)
                sp.wait_ge(stored, 16)

        def act_split(n, slot, half, size):
            nc.scalar.wait_ge(raw_loaded[slot], (half + 1) * 16)
            if not (isinstance(n, int) and n < 2):
                nc.scalar.wait_ge(item_done, n - 1)
            nc.scalar.copy(wh[:, slot, 0:size], raw[:, slot, 0:size]).then_inc(hi_ready, 1)

        def dve_split(n, slot, half, size):
            nc.vector.wait_ge(hi_ready, n + 1)
            nc.vector.tensor_tensor(wl[:, slot, 0:size], raw[:, slot, 0:size], wh[:, slot, 0:size].bitcast(F32),
                                    ALU.subtract).then_inc(lo_ready, 1)

        def ahead(split, n, slot, half, size, j, count):
            if isinstance(j, int) and j == count - 1:
                if n + 1 == len(sizes):
                    return
                size = sizes[n + 1]
            split(n + 1, 1 - slot, half + slot, size)

        class Chain:

            def __init__(self, eng, s):
                self.eng, self.s, self.n = eng, s, 0

            def then(self, ins):
                self.n += 1
                ins.then_inc(self.s, 1)
                self.eng.wait_ge(self.s, self.n)

        @block.gpsimd
        def _(pool):
            pool.wait_ge(x_lo, split_base["mix"] + KD)
            pool.dma_start(mask1[:], t["mask1"]).then_inc(tables1, 16)
            pool.dma_start(rope[:], t["rope"]).then_inc(tables1, 16)
            pool.dma_start(reset[:], t["reset"]).then_inc(tables1, 16)
            for l, norm_name in enumerate(("ln_in", "ln2_0")[:0 if stop == "block1" else 1 if stop == "layer1" else 2]):
                pool.wait_ge(x_lo, split_base[norm_name] + KD)
                pool.dma_start(mask2[:], t["mask2"]).then_inc(tables2, 16)
                pool.dma_start(cmask[:], t["cmask"]).then_inc(tables2, 16)
                pool.dma_start(cmpw[:], t[f"cmpw{l}"]).then_inc(tables2, 16)
            if full:
                pool.wait_ge(n_bias, KD)
                pool.dma_start(mtab[:], t["mtab"]).then_inc(tables3, 16)

        @block.scalar
        def _(act):
            chain = Chain(act, act_chain)
            act_split(0, 0, 0, sizes[0])

            def norm_stats(name):
                i, lns, kind, _, _ = norm_index[name]
                act.preload_act_table_set(LN_EXP)
                for k in range(KD):
                    if kind == "ln":
                        act.wait_ge(n_ctr, 8 * lns + k + 1)
                    if k >= 4 or i > 0:
                        act.wait_ge(n_stat, 8 * i + k - 3)
                    nc.scalar.activation(sq[:, k % 4], xT[:, k], ACT.Square).then_inc(n_sq, 1)
                act.wait_ge(n_stat, 8 * (i + 1))
                chain.then(nc.scalar.activation(rstd[:], ps[:, 0], ACT.Ln, bias=LN_EPS if kind == "ln" else EPS))
                nc.scalar.activation(rstd[:], rstd[:], ACT.Exp, scale=-0.5).then_inc(n_rstd, 1)

            def norm_hi(name, base):
                i, lns, kind, _, b = norm_index[name]
                for k in range(KD):
                    act.wait_ge(n_out, 8 * i + k + 1)
                    if name not in split_base:
                        nc.scalar.activation(xT[:, k], xT[:, k], ACT.Identity, bias=vec(b)[:, k:k + 1]).then_inc(n_bias, 1)
                        continue
                    if kind == "ln":
                        chain.then(nc.scalar.activation(xT[:, k], xT[:, k], ACT.Identity, bias=vec(b)[:, k:k + 1]))
                        src = xT[:, k]
                    else:
                        src = normed[:, k % 2]
                    if name in split_base:
                        nc.scalar.copy(xh[:, k], src).then_inc(x_hi, 1)

            def ffn(name, ups):
                for part, count in enumerate(FF_PARTS):
                    n0 = first[f"{name}_up{part}"]
                    u0 = ups + (FF_PARTS[0] if part else 0)

                    def up(n, slot, half, j):
                        ahead(act_split, n, slot, half, ITEM, j, count)
                        bank = 4 * slot
                        act.wait_ge(item_done, n + 1)
                        nc.scalar.activation(silu_t[:, slot], ps[:, bank], ACT.Silu).then_inc(silu_ready, 1)
                        act.wait_ge(evac_done, n + 1)
                        dst = ah[:, j] if isinstance(j, int) else ah[:, bass.ds(j, 1)].rearrange("p o s -> p (o s)")
                        nc.scalar.copy(dst, gated[:, slot]).then_inc(hidden_hi, 1)

                    item_loop(act, n0, count, up, peel_last=True)
                    size = 2 * count * TILE
                    item_loop(act, first[f"{name}_down{part}"], 4,
                              lambda n, slot, half, j: ahead(act_split, n, slot, half, size, j, 4), peel_last=True)

            def plain_items(stage, count):
                item_loop(act, first[stage], count,
                          lambda n, slot, half, j: ahead(act_split, n, slot, half, ITEM, j, count), peel_last=True)

            act.wait_ge(consts_loaded, 32)
            act.wait_ge(x_loaded, 16)
            norm_stats("ffn1")
            norm_hi("ffn1", 0)
            ffn("ffn1", 0)
            act.wait_ge(evac_done, first["in0"])
            norm_stats("mix")
            norm_hi("mix", 8)
            plain_items("in0", NQKV // 2)
            for j in range(4):
                n = first["tok0"] + j
                ahead(act_split, n, n % 2, n // 2, ITEM, j, 4)
                act_gates(act, j)
            act_block1_mixer(act, chain)
            plain_items("out0", 4)
            act.wait_ge(evac_done, first["ffn2_up0"])
            norm_stats("ffn2")
            norm_hi("ffn2", split_base["ffn2"])
            ffn("ffn2", FF)

            def post_norm(name, done):
                act.wait_ge(evac_done, done)
                norm_stats(name)
                norm_hi(name, split_base.get(name))

            if stop == "block1":
                return
            post_norm("ln_in", first["in1"])
            plain_items("in1", NQKV // 2)
            act_mixer(act, chain, 0)
            plain_items("out1", 4)
            post_norm("ln1_0", first["ffn3_up0"])
            ffn("ffn3", 2 * FF)
            post_norm("ln2_0", first.get("in2", len(sizes)))
            if full:
                plain_items("in2", NQKV // 2)
                act_mixer(act, chain, 1)
                plain_items("out2", 4)
                post_norm("ln1_1", len(sizes))
                act_moe(act, chain)

        @block.vector
        def _(dve):
            chain = Chain(dve, dve_chain)
            dve_split(0, 0, 0, sizes[0])

            def norm(name, base, split=True):
                i, lns, kind, g, _ = norm_index[name]
                if kind == "ln":
                    dve.wait_ge(n_mean, lns + 1)
                    for k in range(KD):
                        nc.vector.tensor_tensor(xT[:, k], xT[:, k], ps[:, 1], ALU.subtract).then_inc(n_ctr, 1)
                    dve.wait_ge(n_ctr, 8 * (lns + 1))
                dve.wait_ge(n_rstd, i + 1)

                def low(k):
                    dve.wait_ge(x_hi, base + k + 1)
                    src = xT[:, k] if kind == "ln" else normed[:, k % 2]
                    nc.vector.tensor_tensor(xl[:, k], src, xh[:, k].bitcast(F32), ALU.subtract).then_inc(x_lo, 1)

                for k in range(KD):
                    dst = xT[:, k] if kind == "ln" else normed[:, k % 2]
                    if kind == "rms" and k >= 2:
                        dve.wait_ge(x_lo, base + k - 1)
                    nc.vector.scalar_tensor_tensor(dst, xT[:, k], vec(g)[:, k:k + 1], rstd[:], ALU.mult,
                                                   ALU.mult).then_inc(n_out, 1)
                    if split and k >= 1:
                        low(k - 1)
                if split:
                    low(KD - 1)

            def ffn(name, ups, old, new):
                for part, count in enumerate(FF_PARTS):
                    n0 = first[f"{name}_up{part}"]
                    u0 = ups + (FF_PARTS[0] if part else 0)

                    def up(n, slot, half, j):
                        ahead(dve_split, n, slot, half, ITEM, j, count)
                        u = j + u0
                        dve.wait_ge(silu_ready, u + 1)
                        if not (isinstance(u, int) and u < 2):
                            dve.wait_ge(hidden_lo, u - 1)
                        nc.vector.tensor_tensor(gated[:, slot], silu_t[:, slot], ps[:, 4 * slot + 1],
                                                ALU.mult).then_inc(evac_done, 1)
                        dve.wait_ge(hidden_hi, u + 1)
                        if isinstance(j, int):
                            hi, lo = ah[:, j], al[:, j]
                        else:
                            hi, lo = (a[:, bass.ds(j, 1)].rearrange("p o s -> p (o s)") for a in (ah, al))
                        nc.vector.tensor_tensor(lo, gated[:, slot], hi.bitcast(F32),
                                                ALU.subtract).then_inc(hidden_lo, 1)

                    item_loop(dve, n0, count, up, peel_last=True)
                    size = 2 * count * TILE
                    item_loop(dve, first[f"{name}_down{part}"], 4, lambda n, slot, half, j: (
                        ahead(dve_split, n, slot, half, size, j, 4),
                        add_to_x(n, slot, j, old if part == 0 else 1.0, new)), peel_last=True)

            def add_to_x(n, slot, j, old, new):
                dve.wait_ge(item_done, n + 1)
                x2 = xT[:, 2 * j:2 * j + 2] if isinstance(j, int) else xT[:, bass.ds(j * 2, 2)]
                x2 = x2.rearrange("p c s -> p (c s)")
                new2 = ps[:, 4 * slot:4 * slot + 2].rearrange("p c s -> p (c s)")
                if old == 1.0:
                    ins = nc.vector.scalar_tensor_tensor(x2, new2, new, x2, ALU.mult, ALU.add)
                else:
                    assert new == 1.0
                    ins = nc.vector.scalar_tensor_tensor(x2, x2, old, new2, ALU.mult, ALU.add)
                ins.then_inc(evac_done, 1)

            def project(stage, count):
                def step(n, slot, half, j):
                    ahead(dve_split, n, slot, half, ITEM, j, count)
                    dve.wait_ge(item_done, n + 1)
                    dst = proj[:, 2 * j:2 * j + 2] if isinstance(j, int) else proj[:, bass.ds(j * 2, 2)]
                    nc.vector.tensor_copy(dst.rearrange("p c s -> p (c s)"),
                                          ps[:, 4 * slot:4 * slot + 2].rearrange("p c s -> p (c s)")).then_inc(evac_done, 1)
                item_loop(dve, first[stage], count, step, peel_last=True)

            def out_items(stage, old):
                item_loop(dve, first[stage], 4, lambda n, slot, half, j: (
                    ahead(dve_split, n, slot, half, ITEM, j, 4), add_to_x(n, slot, j, old, 1.0)), peel_last=True)

            dve.wait_ge(consts_loaded, 32)
            dve.wait_ge(x_loaded, 16)
            norm("ffn1", 0)
            ffn("ffn1", 0, 1.0, 0.5)
            dve.wait_ge(evac_done, first["in0"])
            norm("mix", 8)
            project("in0", NQKV // 2)
            for j in range(4):
                n = first["tok0"] + j
                slot = n % 2
                ahead(dve_split, n, slot, n // 2, ITEM, j, 4)
                if j == 0:
                    dve.wait_ge(evac_done, first["tok0"])
                dve_gates(dve, chain, j)
                dve.wait_ge(item_done, n + 1)
                dst = (vtok if j < 2 else itok)[:, j % 2].rearrange("p t c -> p (t c)")
                nc.vector.tensor_copy(dst, ps[:, 4 * slot:4 * slot + 2].rearrange("p c s -> p (c s)")).then_inc(evac_done, 1)
            dve_block1_mixer(dve, chain)
            out_items("out0", 1.0)
            dve.wait_ge(evac_done, first["ffn2_up0"])
            norm("ffn2", split_base["ffn2"])
            ffn("ffn2", FF, 1.0, 0.5)

            def post_norm(name, done):
                dve.wait_ge(evac_done, done)
                norm(name, split_base.get(name), name in split_base)

            if stop == "block1":
                return
            post_norm("ln_in", first["in1"])
            project("in1", NQKV // 2)
            dve_mixer(dve, chain, 0)
            out_items("out1", ALPHA)
            post_norm("ln1_0", first["ffn3_up0"])
            ffn("ffn3", 2 * FF, ALPHA, 1.0)
            post_norm("ln2_0", first.get("in2", len(sizes)))
            if full:
                project("in2", NQKV // 2)
                dve_mixer(dve, chain, 1)
                out_items("out2", ALPHA)
                post_norm("ln1_1", len(sizes))
                dve_moe(dve, chain)

        @block.tensor
        def _(pe):
            def split_product(dst, hi_w, lo_w, hi_x, lo_x, k, last_k):
                nc.tensor.matmul(dst, hi_w, hi_x, start=(k == 0), stop=False)
                nc.tensor.matmul(dst, hi_w, lo_x, start=False, stop=False)
                return nc.tensor.matmul(dst, lo_w, hi_x, start=False, stop=(k == last_k))

            def wait_item(n):
                pe.wait_ge(lo_ready, n + 1)
                if not (isinstance(n, int) and n < 2):
                    pe.wait_ge(evac_done, n - 1)

            def norm(name):
                i, lns, kind, _, _ = norm_index[name]
                if kind == "ln":
                    for k in range(KD):
                        mm = nc.tensor.matmul(ps[:, 1], consts[:, ONES_D:ONES_D + P], xT[:, k], start=(k == 0), stop=(k == KD - 1))
                    mm.then_inc(n_mean, 1)
                for k in range(KD):
                    pe.wait_ge(n_sq, 8 * i + k + 1)
                    nc.tensor.matmul(ps[:, 0], consts[:, ONES_D:ONES_D + P], sq[:, k % 4], start=(k == 0),
                                     stop=(k == KD - 1)).then_inc(n_stat, 1)

            def columns(stage, count, chunks, hi_x, lo_x, ready, base, order=None):
                order = order or range(chunks)

                def step(n, slot, half, j):
                    wait_item(n)
                    eager = isinstance(j, int) and j == 0
                    for i, k in enumerate(order) if eager else ():
                        pe.wait_ge(ready, base + i + 1)
                        for m in range(2):
                            tile = slice((m * chunks + k) * TILE, (m * chunks + k + 1) * TILE)
                            mm = split_product(ps[:, 4 * slot + m], wh[:, slot, tile], wl[:, slot, tile],
                                               hi_x[:, k], lo_x[:, k], i, chunks - 1)
                    for m in range(2) if not eager else ():
                        for k in range(chunks):
                            tile = slice((m * chunks + k) * TILE, (m * chunks + k + 1) * TILE)
                            mm = split_product(ps[:, 4 * slot + m], wh[:, slot, tile], wl[:, slot, tile],
                                               hi_x[:, k], lo_x[:, k], k, chunks - 1)
                    mm.then_inc(item_done, 1)
                item_loop(pe, first[stage], count, step, peel_first=True)

            def tokens(n, width):
                slot = n % 2
                wait_item(n)
                for tt in range(NT):
                    if width == 256:
                        dst = ps[:, 4 * slot + tt // 2, (tt % 2) * 256:(tt % 2) * 256 + 256]
                    else:
                        dst = ps[:, 4 * slot + tt, 0:width]
                    tok = slice(tt * P, (tt + 1) * P)
                    for k in range(KD):
                        cols = slice(k * width, (k + 1) * width)
                        nc.tensor.matmul(dst, xh[:, k, tok], wh[:, slot, cols], start=(k == 0), stop=False)
                        nc.tensor.matmul(dst, xh[:, k, tok], wl[:, slot, cols], start=False, stop=False)
                        mm = nc.tensor.matmul(dst, xl[:, k, tok], wh[:, slot, cols], start=False, stop=(k == KD - 1))
                mm.then_inc(item_done, 1)

            def ffn(name, split, ups):
                for part, count in enumerate(FF_PARTS):
                    columns(f"{name}_up{part}", count, KD, xh, xl, x_lo, split_base[split])
                    columns(f"{name}_down{part}", 4, count, ah, al, hidden_lo, ups)
                    ups += count

            pe.wait_ge(consts_loaded, 32)
            pe.wait_ge(x_loaded, 16)
            norm("ffn1")
            ffn("ffn1", "ffn1", 0)
            pe.wait_ge(evac_done, first["in0"])
            norm("mix")
            columns("in0", NQKV // 2, KD, xh, xl, x_lo, split_base["mix"])
            for j in range(4):
                tokens(first["tok0"] + j, 256)
            pe_block1_mixer(pe)
            columns("out0", 4, KD, xh, xl, x_lo, split_base["mixed0"])
            pe.wait_ge(evac_done, first["ffn2_up0"])
            norm("ffn2")
            ffn("ffn2", "ffn2", FF)

            def post_norm(name, done):
                pe.wait_ge(evac_done, done)
                norm(name)

            if stop == "block1":
                return
            post_norm("ln_in", first["in1"])
            columns("in1", NQKV // 2, KD, xh, xl, x_lo, split_base["ln_in"])
            tokens(first["tok1"], 280)
            pe_mixer(pe, 0)
            columns("out1", 4, KD, xh, xl, x_lo, split_base["mixed1"], MIXED_ORDER)
            post_norm("ln1_0", first["ffn3_up0"])
            ffn("ffn3", "ln1_0", 2 * FF)
            post_norm("ln2_0", first.get("in2", len(sizes)))
            if full:
                columns("in2", NQKV // 2, KD, xh, xl, x_lo, split_base["ln2_0"])
                tokens(first["tok2"], 280)
                pe_mixer(pe, 1)
                columns("out2", 4, KD, xh, xl, x_lo, split_base["mixed2"], MIXED_ORDER)
                post_norm("ln1_1", len(sizes))
                pe_moe(pe)


def up_layout(w1, w3):
    a = np.stack([w1, w3]).reshape(2, KD, P, -1, P)
    return np.ascontiguousarray(a.transpose(3, 2, 0, 1, 4)).reshape(a.shape[3], P, ITEM)


def column_layout(w):
    k, m = w.shape
    a = w.reshape(k // P, P, m // (2 * P), 2, P)
    return np.ascontiguousarray(a.transpose(2, 1, 3, 0, 4)).reshape(m // (2 * P), P, 2 * k)


def token_layout(w, width):
    a = w.reshape(KD, P, -1, width)
    return np.ascontiguousarray(a.transpose(2, 1, 0, 3)).reshape(a.shape[2], P, KD * width)


def shape_constants():
    p = np.arange(P)[:, None]
    q = np.arange(P)[None, :]
    consts = np.zeros((P, NCONST), np.float32)
    consts[:, IDENT:IDENT + P] = p == q
    consts[:, ONES_D:ONES_D + P] = 1.0 / D
    consts[:, ONES_H:ONES_H + P] = (p // HD == q // HD) / HD
    half = HD // 8
    d = q % HD
    partner = np.where(d < half, q + half, q - half)
    consts[:, ROT:ROT + P] = (p == partner) & (d < 2 * half)
    for g, at in enumerate((SEL0, SEL1)):
        consts[:, at:at + P] = p == g * HD + q % HD
    consts[:, HMASK:HMASK + P] = ((p // CHUNK == q // CHUNK) & (p <= q)).astype(np.int32).view(np.float32)
    dist = (np.arange(S)[None, :] * -1 + (S - P) + p)
    count = (dist <= 128) * 1 + (dist % 4 == 0) * 1 + (dist % 16 == 0) * 1
    count = np.where(dist >= 0, count, 0)
    logc = np.log(np.maximum(count, 1).astype(np.float64)) / SCALE
    mask1 = np.where(count > 0, logc, NEG / SCALE).astype(np.float32)
    mask2 = np.where(dist >= 0, 0.0, NEG / SCALE).astype(np.float32)
    inv = np.float32(500000.0) ** (-np.arange(0, 16, 2, dtype=np.float32) / np.float32(16))
    ang = (np.arange(S, dtype=np.float32)[:, None] * inv[None, :]).astype(np.float32)
    cos, sin = np.cos(ang).T, np.sin(ang).T
    rope = np.zeros((P, 2, S), np.float32)
    rope[:, 0] = 1.0
    for h in range(2):
        for i in range(half):
            rope[h * HD + i, 0], rope[h * HD + half + i, 0] = cos[i], cos[i]
            rope[h * HD + i, 1], rope[h * HD + half + i, 1] = -sin[i], sin[i]
    reset = np.ones((P, S), np.float32)
    reset[:, ::CHUNK] = 0.0
    tok = np.arange(NT)[None, :, None] * P + p[:, :, None]
    seen = 16 * np.arange(NCMP)[None, None, :] + 31 <= tok
    cmask = np.stack([np.where(seen, 0.0, NEG), seen], axis=1).reshape(P, 2, NT * NCMP).astype(np.float32)
    return {"cmask": cmask, "consts": consts, "mask1": mask1, "mask2": mask2, "rope": rope, "reset": reset}


def lay_out(i, stop):
    def cols(w):
        return w.reshape(-1, P).T

    x = np.asarray(i["x"]).reshape(S, D)
    t = {"xT": np.ascontiguousarray(x.T.reshape(KD, P, S).transpose(1, 0, 2))}
    c = shape_constants()
    v = np.zeros((P, NVEC), np.float32)

    def put(name, block):
        at, n = VCOL[name]
        v[:, at:at + n] = block

    for name in ("ffn1_norm", "mix_norm", "ffn2_norm"):
        put(name, cols(i[name]))
    put("q_norm", np.concatenate([i["q_norm"][0]] * 2)[:, None])
    put("k_norm", np.concatenate([i["k_norm"][0]] * 2)[:, None])
    put("hg_out_norm", cols(i["hg_out_norm"]))
    put("lb_logits", cols(i["hg_lb_logits"]))
    t["vecs"] = v
    for k in ("consts", "mask1", "rope", "reset"):
        t[k] = c[k]
    for name in ("ffn1", "ffn2"):
        t[f"{name}_up"] = up_layout(i[f"{name}_w1"][0], i[f"{name}_w3"][0])
        cut = FF_PARTS[0] * P
        t[f"{name}_down0"] = column_layout(i[f"{name}_w2"][0][:cut])
        t[f"{name}_down1"] = column_layout(i[f"{name}_w2"][0][cut:])
    w = i["w_in"][0]
    t["in0"] = column_layout(np.concatenate([w[:, 0:1024], w[:, 1536:2560], w[:, 3072:3584]], axis=1))
    t["tok0"] = token_layout(np.concatenate([w[:, 1024:1536], w[:, 2560:3072]], axis=1), 256)
    t["out0"] = column_layout(i["w_out"][0])
    if stop == "block1":
        return t
    put("ln_in_g", cols(i["ln_in_g_2"]))
    put("ln_in_b", cols(i["ln_in_b_2"]))
    t["mask2"], t["cmask"] = c["mask2"], c["cmask"]
    for l in range(2 if stop == "all" else 1):
        for name in ("ln1_g", "ln1_b", "ln2_g", "ln2_b"):
            put(f"{name}{l}", cols(i[f"{name}_2"][l]))
        put(f"conv{l}", cols(i["conv_w_2"][l]))
        put(f"cmp_b1{l}", cols(i["cmp_b1_2"][l]))
        put(f"cmp_b2k{l}", np.concatenate([i["cmp_b2_2"][l, 0]] * 2)[:, None])
        w = i["w_in_2"][l]
        kc, vc, ks, vs, kw, vw = (w[:, 512 + P * n:640 + P * n] for n in range(6))
        t[f"in{l + 1}"] = column_layout(np.concatenate([w[:, 0:512], kc, vc, ks, kw, w[:, 1304:]], axis=1))
        t[f"tok{l + 1}"] = token_layout(np.concatenate([vs, vw, w[:, 1280:1304]], axis=1), 280)
        t[f"cmp{l + 1}"] = np.ascontiguousarray(
            i["cmp_w1_2"][l].reshape(4, 8, P, 256).transpose(0, 2, 1, 3)).reshape(4, P, ITEM)
        t[f"out{l + 1}"] = column_layout(i["w_o_2"][l])
        small = np.zeros((P, 480), np.float32)
        w2 = i["cmp_w2_2"][l].reshape(2, 2, P, HD).transpose(0, 2, 1, 3)
        small[:, 0:256] = np.concatenate([w2[0], w2[0]], axis=2).reshape(P, 256)
        small[:, 256:384] = w2[1].reshape(P, P)
        small[:, 384:448] = i["cmp_b2_2"][l, 1][None, :]
        small[:, 448:480] = i["cmp_pos_2"][l].reshape(2, 16, P).transpose(2, 0, 1).reshape(P, 32)
        t[f"cmpw{l}"] = small
    t["ffn3_up"] = up_layout(i["ffn_wg_2"][0], i["ffn_wu_2"][0])
    t["ffn3_down0"] = column_layout(i["ffn_wd_2"][0][:cut])
    t["ffn3_down1"] = column_layout(i["ffn_wd_2"][0][cut:])
    if stop != "all":
        return t
    tab = np.zeros((P, WIDE + 2 * P + NE + KD * NE), np.float32)
    tab[:, 0:WIDE] = np.arange(WIDE)
    tab[:, WIDE:WIDE + P] = np.arange(P)[:, None] < np.arange(P)[None, :]
    tab[:, WIDE + P:WIDE + 2 * P] = 1.0
    tab[:, WIDE + 2 * P:WIDE + 2 * P + NE] = np.arange(NE)
    tab[:, WIDE + 2 * P + NE:] = i["moe_router_2"][0].reshape(KD, P, NE).transpose(1, 0, 2).reshape(P, KD * NE)
    t["mtab"] = tab
    t["lastrow"] = np.stack([i["ln2_g_2"][1], i["ln2_b_2"][1]]).reshape(1, 2 * D)
    t["moe_up"] = np.concatenate([up_layout(g, u) for g, u in zip(i["moe_wg_2"][0], i["moe_wu_2"][0])])
    t["moe_down"] = np.ascontiguousarray(
        i["moe_wd_2"][0].reshape(NE, FE, P, KD, P).transpose(0, 3, 2, 1, 4)).reshape(NE * KD, P, FE * TILE)
    return t


def kernel(**inputs):
    import concourse.bacc as bacc
    from concourse.bass_utils import run_bass_kernel_spmd

    t = lay_out({k: np.asarray(v) for k, v in inputs.items()}, STOP)
    nc = bacc.Bacc("TRN2", target_bir_lowering=False, num_devices=1)
    aps = {k: nc.dram_tensor(f"in_{k}", a.shape, mybir.dt.from_np(a.dtype), kind="ExternalInput").ap() for k, a in t.items()}
    shape = (S, D) if STOP == "all" else (P, KD, S)
    out = nc.dram_tensor("out", shape, F32, kind="ExternalOutput").ap()
    build(nc, aps, out, STOP)
    got = run_bass_kernel_spmd(nc, [{f"in_{k}": a for k, a in t.items()}], core_ids=[0]).results[0]["out"]
    return got.reshape(1, S, D) if STOP == "all" else got


STOP = "all"
```
